# Optimizing a Trainium2 kernel written in Bass

```python
import jax, jax.numpy as jnp
from jax import lax
import numpy as np

D_MODEL = 1024
BATCH = 1
SEQ = 512
DEPTH = 1
DEC_BATCH = 1
DEC_SEQ = 1024
PAST_LEN = 128

A_WIDTH = D_MODEL
A_GROUPS = 8
A_GROUP_CH = A_WIDTH // A_GROUPS
CHUNK = 128
HEAD_DIM = 128
N_Q_HEADS = D_MODEL // HEAD_DIM
N_KV_HEADS = 2
WINDOW = 128
BLOCK = 128
ROPE_THETA = 10000.0
Q_W = N_Q_HEADS * HEAD_DIM
KV_W = N_KV_HEADS * HEAD_DIM
IN_W = 2 * A_WIDTH + Q_W + 2 * KV_W + 2 * D_MODEL
SPLITS = (A_WIDTH, 2 * A_WIDTH, 2 * A_WIDTH + Q_W, 2 * A_WIDTH + Q_W + KV_W,
          2 * A_WIDTH + Q_W + 2 * KV_W, 2 * A_WIDTH + Q_W + 2 * KV_W + D_MODEL)
N_GROUPS = 4
EXPERTS_PER_GROUP = 8
N_EXPERTS = N_GROUPS * EXPERTS_PER_GROUP
TOP_K = 2
D_EXPERT = 512
MOE_BLOCK = 128
EPS = 1e-6
NEG = -1e30

kernel_name = "hybrid_sgmlp_swa_hmoe_encoder"

def rms_norm(x, g):
    xf = x.astype(jnp.float32)
    y = xf * lax.rsqrt(jnp.mean(xf * xf, axis=-1, keepdims=True) + EPS)
    return (y * g.astype(jnp.float32)).astype(x.dtype)

def apply_rope(x, pos):
    half = HEAD_DIM // 2
    inv_freq = ROPE_THETA ** (-jnp.arange(half, dtype=jnp.float32) / half)
    ang = pos.astype(jnp.float32)[:, None] * inv_freq[None, :]
    cos = jnp.cos(ang)[None, :, None, :]
    sin = jnp.sin(ang)[None, :, None, :]
    xf = x.astype(jnp.float32)
    x1, x2 = xf[..., :half], xf[..., half:]
    return jnp.concatenate([x1 * cos - x2 * sin, x2 * cos + x1 * sin], axis=-1).astype(x.dtype)

def spatial_gating_mixer(u, v, norm_v_g, w_spatial, b_spatial):
    B, S, _ = u.shape
    u = jax.nn.gelu(u)
    v = rms_norm(jax.nn.gelu(v), norm_v_g)
    vc = v.reshape(B, S // CHUNK, CHUNK, A_GROUPS, A_GROUP_CH)
    mixed = jnp.einsum('gpq,bnqgc->bnpgc', w_spatial, vc) + b_spatial.T[None, None, :, :, None]
    return u * mixed.reshape(B, S, A_WIDTH)

def window_attention(q, k, v, q_norm_g, k_norm_g, sink):
    B, S, _ = q.shape
    rep = N_Q_HEADS // N_KV_HEADS
    pos = jnp.arange(S)
    q = apply_rope(rms_norm(q.reshape(B, S, N_Q_HEADS, HEAD_DIM), q_norm_g), pos)
    k = apply_rope(rms_norm(k.reshape(B, S, N_KV_HEADS, HEAD_DIM), k_norm_g), pos)
    v = v.reshape(B, S, N_KV_HEADS, HEAD_DIM)
    n_blk = S // BLOCK
    qb = q.reshape(B, n_blk, BLOCK, N_KV_HEADS, rep, HEAD_DIM).transpose(1, 0, 2, 3, 4, 5)
    pad = ((0, 0), (BLOCK, BLOCK), (0, 0), (0, 0))
    kp = jnp.pad(k, pad)
    vp = jnp.pad(v, pad)
    q_off = jnp.arange(BLOCK)
    k_off = jnp.arange(3 * BLOCK) - BLOCK
    band = jnp.abs(k_off[None, :] - q_off[:, None]) <= WINDOW
    scale = HEAD_DIM ** -0.5
    sink_l = jnp.broadcast_to(sink.astype(jnp.float32).reshape(1, N_KV_HEADS, rep, 1, 1),
                              (B, N_KV_HEADS, rep, BLOCK, 1))

    def one_block(args):
        qi, i = args
        ki = lax.dynamic_slice_in_dim(kp, i * BLOCK, 3 * BLOCK, axis=1)
        vi = lax.dynamic_slice_in_dim(vp, i * BLOCK, 3 * BLOCK, axis=1)
        kpos = i * BLOCK + k_off
        valid = band & ((kpos >= 0) & (kpos < S))[None, :]
        s = jnp.einsum('bqgrd,bkgd->bgrqk', qi, ki).astype(jnp.float32) * scale
        s = jnp.where(valid, s, NEG)
        p = jax.nn.softmax(jnp.concatenate([s, sink_l], axis=-1), axis=-1)[..., :-1]
        o = jnp.einsum('bgrqk,bkgd->bqgrd', p.astype(vi.dtype), vi)
        return o.reshape(B, BLOCK, Q_W)

    out = lax.map(one_block, (qb, jnp.arange(n_blk)))
    return out.transpose(1, 0, 2, 3).reshape(B, S, Q_W)

def hierarchical_moe(h, w_rg, b_rg, w_re, b_re, w_gate, w_up, w_down):
    B, S, D = h.shape
    T = B * S
    xf = h.reshape(T, D)
    g_logits = (xf @ w_rg).astype(jnp.float32) + b_rg.astype(jnp.float32)
    g_prob = jax.nn.softmax(g_logits, axis=-1)
    g_sel = jnp.argmax(g_logits, axis=-1)
    g_p = jnp.take_along_axis(g_prob, g_sel[:, None], axis=1)
    e_logits = ((xf @ w_re).astype(jnp.float32) + b_re.astype(jnp.float32)).reshape(T, N_GROUPS, EXPERTS_PER_GROUP)
    e_logits = jnp.take_along_axis(e_logits, g_sel[:, None, None], axis=1)[:, 0]
    e_prob = jax.nn.softmax(e_logits, axis=-1)
    top_p, top_e = lax.top_k(e_prob, TOP_K)
    gates = g_p * top_p / jnp.sum(top_p, axis=-1, keepdims=True)
    expert_id = (g_sel[:, None] * EXPERTS_PER_GROUP + top_e).astype(jnp.int32)

    A = T * TOP_K
    flat_e = expert_id.reshape(A)
    flat_w = gates.reshape(A)
    flat_tok = (jnp.arange(A) // TOP_K).astype(jnp.int32)
    order = jnp.argsort(flat_e)
    sorted_e = flat_e[order]
    counts = jnp.bincount(flat_e, length=N_EXPERTS).astype(jnp.int32)
    starts = jnp.cumsum(counts) - counts
    padded = (counts + MOE_BLOCK - 1) // MOE_BLOCK * MOE_BLOCK
    pad_ends = jnp.cumsum(padded)
    pad_starts = pad_ends - padded
    dest = pad_starts[sorted_e] + jnp.arange(A, dtype=jnp.int32) - starts[sorted_e]
    n_blocks = -(-A // MOE_BLOCK) + N_EXPERTS
    P = n_blocks * MOE_BLOCK
    slot_tok = jnp.full((P,), T, jnp.int32).at[dest].set(flat_tok[order])
    slot_w = jnp.zeros((P,), h.dtype).at[dest].set(flat_w[order].astype(h.dtype))
    block_start = jnp.arange(n_blocks, dtype=jnp.int32) * MOE_BLOCK
    block_e = jnp.minimum(jnp.searchsorted(pad_ends, block_start, side='right'), N_EXPERTS - 1)
    xpad = jnp.concatenate([xf, jnp.zeros((1, D), xf.dtype)], axis=0)
    xb = xpad[slot_tok].reshape(n_blocks, MOE_BLOCK, D)

    def expert_block(args):
        xblk, e = args
        hid = jax.nn.silu(xblk @ w_gate[e]) * (xblk @ w_up[e])
        return hid @ w_down[e]

    yb = lax.map(expert_block, (xb, block_e)).reshape(P, D)
    y = jnp.zeros((T + 1, D), h.dtype).at[slot_tok].add(yb * slot_w[:, None])
    return y[:T].reshape(B, S, D)

def encoder_layer(x, norm_mix_g, w_in, norm_v_g, w_spatial, b_spatial, q_norm_g, k_norm_g, sink,
                  w_proj_a, w_proj_b, w_out, norm_ffn_g, w_router_group, b_router_group,
                  w_router_expert, b_router_expert, w_gate_e, w_up_e, w_down_e):
    h = rms_norm(x, norm_mix_g)
    z = h @ w_in
    u, v, q, k, va, gate_a, gate_b = jnp.split(z, SPLITS, axis=-1)
    ya = spatial_gating_mixer(u, v, norm_v_g, w_spatial, b_spatial) @ w_proj_a
    yb = window_attention(q, k, va, q_norm_g, k_norm_g, sink) @ w_proj_b
    merged = jax.nn.sigmoid(gate_a) * ya + jax.nn.sigmoid(gate_b) * yb
    x = x + merged @ w_out
    x = x + hierarchical_moe(rms_norm(x, norm_ffn_g), w_router_group, b_router_group,
                             w_router_expert, b_router_expert, w_gate_e, w_up_e, w_down_e)
    return x

def setup_inputs(seed: int = 0) -> dict:
    key = jax.random.key(seed)
    ks = jax.random.split(key, 24)
    f32 = jnp.float32
    L = DEPTH

    def nrm(k, shape, scale):
        return jax.random.normal(k, shape, f32) * scale

    def gain(k, shape):
        return 1.0 + 0.01 * jax.random.normal(k, shape, f32)

    return {
        "x_prompt": nrm(ks[0], (BATCH, SEQ, D_MODEL), 1.0),
        "x_sample": nrm(ks[1], (DEC_BATCH, DEC_SEQ, D_MODEL), 1.0),
        "norm_mix_g": gain(ks[2], (L, D_MODEL)),
        "w_in": nrm(ks[3], (L, D_MODEL, IN_W), D_MODEL ** -0.5),
        "norm_v_g": gain(ks[4], (L, A_WIDTH)),
        "w_spatial": nrm(ks[5], (L, A_GROUPS, CHUNK, CHUNK), CHUNK ** -0.5),
        "b_spatial": 1.0 + nrm(ks[6], (L, A_GROUPS, CHUNK), 0.02),
        "q_norm_g": gain(ks[7], (L, HEAD_DIM)),
        "k_norm_g": gain(ks[8], (L, HEAD_DIM)),
        "sink": nrm(ks[9], (L, N_Q_HEADS), 0.5),
        "w_proj_a": nrm(ks[10], (L, A_WIDTH, D_MODEL), A_WIDTH ** -0.5),
        "w_proj_b": nrm(ks[11], (L, Q_W, D_MODEL), Q_W ** -0.5),
        "w_out": nrm(ks[12], (L, D_MODEL, D_MODEL), D_MODEL ** -0.5),
        "norm_ffn_g": gain(ks[13], (L, D_MODEL)),
        "w_router_group": nrm(ks[14], (L, D_MODEL, N_GROUPS), D_MODEL ** -0.5),
        "b_router_group": nrm(ks[15], (L, N_GROUPS), 0.01),
        "w_router_expert": nrm(ks[16], (L, D_MODEL, N_EXPERTS), D_MODEL ** -0.5),
        "b_router_expert": nrm(ks[17], (L, N_EXPERTS), 0.01),
        "w_gate_e": nrm(ks[18], (L, N_EXPERTS, D_MODEL, D_EXPERT), D_MODEL ** -0.5),
        "w_up_e": nrm(ks[19], (L, N_EXPERTS, D_MODEL, D_EXPERT), D_MODEL ** -0.5),
        "w_down_e": nrm(ks[20], (L, N_EXPERTS, D_EXPERT, D_MODEL), D_EXPERT ** -0.5),
    }

def reference(x_prompt, x_sample, norm_mix_g, w_in, norm_v_g, w_spatial, b_spatial, q_norm_g,
              k_norm_g, sink, w_proj_a, w_proj_b, w_out, norm_ffn_g, w_router_group,
              b_router_group, w_router_expert, b_router_expert, w_gate_e, w_up_e, w_down_e):
    def trunk(x):
        for l in range(DEPTH):
            x = encoder_layer(x, norm_mix_g[l], w_in[l], norm_v_g[l], w_spatial[l], b_spatial[l],
                              q_norm_g[l], k_norm_g[l], sink[l], w_proj_a[l], w_proj_b[l],
                              w_out[l], norm_ffn_g[l], w_router_group[l], b_router_group[l],
                              w_router_expert[l], b_router_expert[l], w_gate_e[l], w_up_e[l],
                              w_down_e[l])
        return x

    y_prompt = trunk(x_prompt)
    y_sample = trunk(x_sample)
    return (y_prompt, y_sample)


_drawn_inputs = setup_inputs


def setup_inputs(seed=0):
    import zlib

    import numpy as np

    out = dict(_drawn_inputs(seed))
    spreads = {}
    factors = {'norm_mix_g': 2.896,
     'norm_v_g': 4.546,
     'b_spatial': 3.83,
     'q_norm_g': 8.0,
     'k_norm_g': 8.0,
     'sink': 8.0,
     'norm_ffn_g': 2.959,
     'b_router_group': 26.302,
     'b_router_expert': 3.642}
    for name, (base, spread) in spreads.items():
        noise = np.random.default_rng([zlib.crc32(name.encode()), seed]).standard_normal(out[name].shape)
        drawn = base * np.exp(spread * noise) if base else spread * noise
        out[name] = __import__('jax').numpy.asarray(drawn.astype(out[name].dtype))
    for name, factor in factors.items():
        out[name] = (out[name] * factor).astype(out[name].dtype)
    return out
```

```python
from contextlib import ExitStack

import numpy as np

import concourse.bass as bass
from concourse import mybir

F32 = mybir.dt.float32
F32R = mybir.dt.float32r
I32 = mybir.dt.int32
ALU = mybir.AluOpType
ACT = mybir.ActivationFunctionType
AX_X = mybir.AxisListType.X

P = 128
D = 1024
KT = D // P
HD = 128
NH, NKV = 8, 2
REP = NH // NKV
S_PROMPT, S_SAMPLE = 512, 1024
T = S_PROMPT + S_SAMPLE
G = 512
NG = T // G
GT = G // P
NT = T // P
N_GROUPS, EPG = 4, 8
NE = N_GROUPS * EPG
DE = 512
CAP = T
MAXB = 2 * T // P + NE
NTAB = MAXB + 8
EPS = 1e-6
NEG = -1e30
BIG = 3e38

U0, V0, Q0, K0, VA0, GA0, GB0 = 0, 1024, 2048, 3072, 3328, 3584, 4608
PANELS = [("w_in", K0, 256), ("w_in", VA0, 256), ("w_in", Q0, 512), ("w_in", Q0 + 512, 512),
          ("w_in", GB0, 512), ("w_in", GB0 + 512, 512), ("w_proj_b", 0, 512), ("w_proj_b", 512, 512),
          ("w_in", V0, 512), ("w_in", V0 + 512, 512), ("w_in", U0, 512), ("w_in", U0 + 512, 512),
          ("w_in", GA0, 512), ("w_in", GA0 + 512, 512), ("w_proj_a", 0, 512), ("w_proj_a", 512, 512),
          ("w_out", 0, 512), ("w_out", 512, 512)]
PK, PVA, PQ, PGB, PPB, PV, PU, PGA, PPA, POUT = 0, 1, 2, 4, 6, 8, 10, 12, 14, 16
NP = len(PANELS)
NQ = 4
QPG = NP * NQ
NRAW = 3
NU = NH * GT
SCALE = float(HD) ** -0.5


def mixers(nc, a):
    with ExitStack() as ctx:
        base = nc.sbuf_base + (-nc.sbuf_base) % 64
        arena = {"at": base}

        def place(name, shape, dt, at=None):
            size = int(np.prod(shape[1:])) * 4
            if at is None:
                at = arena["at"]
                arena["at"] += size + (-size) % 32
            return nc.alloc_sbuf_tensor_at(name, shape, dt, offset=at)[...], at

        hT_hi, _ = place("hT_hi", [P, KT, G], F32R)
        hT_lo, _ = place("hT_lo", [P, KT, G], F32R)
        hx_hi, _ = place("hx_hi", [P, KT, P], F32R)
        hx_lo, _ = place("hx_lo", [P, KT, P], F32R)
        w_hi = [place(f"w_hi{i}", [P, KT, 512], F32R)[0] for i in range(2)]
        w_lo = [place(f"w_lo{i}", [P, KT, 512], F32R)[0] for i in range(2)]
        raw = [place(f"raw{i}", [P, 1024], F32)[0] for i in range(NRAW)]
        kT, _ = place("kT", [P, NKV, 6 * P], F32)
        va, _ = place("va", [P, 6, NKV * HD], F32)
        A, B, C, Dd = (place(f"region{i}", [P, 4096], F32)[1] for i in range(4))
        T1, T2 = (place(f"temp{i}", [P, 1024], F32)[1] for i in range(2))
        qT, _ = place("qT", [P, NH, G], F32, A)
        oT_hi, _ = place("oT_hi", [P, NH, G], F32R, A)
        ws, _ = place("ws", [P, NH, P], F32, A)
        vn, _ = place("vn", [P, GT, D], F32, A)
        sga, _ = place("sga", [P, KT, G], F32, A)
        m_lo, _ = place("m_lo", [P, KT, G], F32R, A)
        qn, _ = place("qn", [P, 2, GT, 512], F32, B)
        oT_lo, _ = place("oT_lo", [P, NH, G], F32R, B)
        uT, _ = place("uT", [P, KT, G], F32, B)
        aT_hi, _ = place("aT_hi", [P, KT, G], F32R, B)
        x2, _ = place("x2", [P, GT, D], F32, B)
        sgb, _ = place("sgb", [P, KT, G], F32, C)
        m_hi, _ = place("m_hi", [P, KT, G], F32R, C)
        xn, _ = place("xn", [P, GT, D], F32, Dd)
        kn, _ = place("kn", [P, 5, 256], F32, Dd)
        sq, _ = place("sq", [P, 512], F32, Dd + 5120)
        rot, _ = place("rot", [P, 512], F32, Dd + 7168)
        pt = [place(f"pt{i}", [P, 3 * P], F32, Dd + 1536 * i)[0] for i in range(2)]
        sm = [place("sm0", [P, 3 * P], F32, Dd + 3072)[0], place("sm1", [P, 3 * P], F32, Dd + 9216)[0]]
        pr = [place(f"pr{i}", [P, 3 * P], F32, Dd + 10752 + 1536 * i)[0] for i in range(3)]
        aT_lo, _ = place("aT_lo", [P, KT, G], F32R, Dd)
        xh, _ = place("xh", [P, D], F32, T1)
        bsp, _ = place("bsp", [P, NH, P], F32, T1)
        junk, _ = place("junk", [P, D], F32, T2)
        tmp = [place(f"tmp{i}", [P, G], F32, T2 + 2048 * i)[0] for i in range(2)]
        mask, _ = place("mask", [P, 3, 3 * P], F32)
        rope, _ = place("rope", [P, 5, 2, HD // 2], F32)
        ident, _ = place("ident", [P, P], F32)
        wsT, _ = place("wsT", [P, NH, P], F32)
        gq, _ = place("gq", [P, HD], F32)
        gk, _ = place("gk", [P, HD], F32)
        g_mix, _ = place("g_mix", [P, KT], F32)
        g_v, _ = place("g_v", [P, KT], F32)
        sink, _ = place("sink", [P, NH], F32)
        nsink, _ = place("nsink", [P, NH], F32)
        half, _ = place("half", [P, 8], F32)
        ssx, _ = place("ssx", [P, 8], F32)
        rsx, _ = place("rsx", [P, 8], F32)
        ssq, _ = place("ssq", [P, 8], F32)
        rsq, _ = place("rsq", [P, 8], F32)
        ssv, _ = place("ssv", [P, GT, 2], F32)
        rsv, _ = place("rsv", [P, GT], F32)
        stat, _ = place("stat", [P, 4, 8], F32)
        assert arena["at"] <= nc.sbuf_usable_end, (arena["at"], nc.sbuf_usable_end)

        main = [ctx.enter_context(nc.psum_tensor(f"main{i}", [P, 512], F32)) for i in range(4)]
        aux = [ctx.enter_context(nc.psum_tensor(f"aux{i}", [P, 512], F32)) for i in range(4)]

        def sem(name):
            return ctx.enter_context(nc.semaphore(name))

        raw_in = [sem(f"raw_in{i}") for i in range(NRAW)]
        w_hi_done, w_split, out_ready = sem("w_hi_done"), sem("w_split"), sem("out_ready")
        const_in, const_set, ws_in, ws_ps, ws_done = sem("const_in"), sem("const_set"), sem("ws_in"), sem("ws_ps"), sem("ws_done")
        x_in, xh_in, table_in, bsp_in, x2_in = sem("x_in"), sem("xh_in"), sem("table_in"), sem("bsp_in"), sem("x2_in")
        ssx_ready, rsx_ready, xn_ready, hT_ps, hT_hi_done, hT_done = (
            sem("ssx_ready"), sem("rsx_ready"), sem("xn_ready"), sem("hT_ps"), sem("hT_hi_done"), sem("hT_done"))
        hx_ps, hx_mul, hx_hi_done, hx_done = sem("hx_ps"), sem("hx_mul"), sem("hx_hi_done"), sem("hx_done")
        halo_ready, sq_ready, ssq_ready, rsq_ready, head_normed, head_roped = (
            sem("halo_ready"), sem("sq_ready"), sem("ssq_ready"), sem("rsq_ready"), sem("head_normed"), sem("head_roped"))
        kT_ps, kT_done, va_done, qT_ps, qT_done, halo_kept = (
            sem("kT_ps"), sem("kT_done"), sem("va_done"), sem("qT_ps"), sem("qT_done"), sem("halo_kept"))
        s_ps, s_masked, negm_ready, exp_done, rden_ready, p_ready = (
            sem("s_ps"), sem("s_masked"), sem("negm_ready"), sem("exp_done"), sem("rden_ready"), sem("p_ready"))
        pt_ps, pt_ready, o_ps, o_hi_done, o_done = sem("pt_ps"), sem("pt_ready"), sem("o_ps"), sem("o_hi_done"), sem("o_done")
        tanh_b, sgb_ready, mb_done, tanh_a, sga_ready = sem("tanh_b"), sem("sgb_ready"), sem("mb_done"), sem("tanh_a"), sem("sga_ready")
        gelu_v, ssv_ready, rsv_ready, vn_ready, uT_ready = sem("gelu_v"), sem("ssv_ready"), sem("rsv_ready"), sem("vn_ready"), sem("uT_ready")
        sp_ps, mixed_ready, a_ready, a_hi_done, a_done = sem("sp_ps"), sem("mixed_ready"), sem("a_ready"), sem("a_hi_done"), sem("a_done")
        ya_gated, m_ready, m_hi_done, m_done = sem("ya_gated"), sem("m_ready"), sem("m_hi_done"), sem("m_done")
        x2_done, y_out = sem("x2_done"), sem("y_out")
        pool_step, dve_step, settled = sem("pool_step"), sem("dve_step"), sem("settled")

        def quarter(i):
            p, q = divmod(i % QPG, NQ)
            name, c, n = PANELS[p]
            src = a[name][256 * q:256 * q + 256, c:c + n].rearrange("(k p) c -> p k c", p=P)
            buf = raw[i % NRAW][:, 0:2 * n].rearrange("p (k c) -> p k c", k=2)
            return src, buf, w_hi[p % 2][:, 2 * q:2 * q + 2, 0:n], w_lo[p % 2][:, 2 * q:2 * q + 2, 0:n]

        with nc.Block() as block:

            @block.sync
            def _(sp):
                sp.dma_start(ident, a["ident"]).then_inc(const_in, 16)
                sp.dma_start(g_mix, a["norm_mix_g"]).then_inc(const_in, 16)
                for i in range(NRAW):
                    src, buf, _, _ = quarter(i)
                    sp.dma_start(buf, src).then_inc(raw_in[i], 16)
                sp.dma_start(g_v, a["norm_v_g"]).then_inc(const_in, 16)
                for dst, name, n in ((gq, "q_norm_g", HD), (gk, "k_norm_g", HD), (sink, "sink", NH)):
                    sp.dma_start(dst, a[name].to_broadcast([P, n])).then_inc(const_in, 16)
                with sp.Fori(0, NG) as g:
                    for i in range(QPG):
                        sp.wait_ge(w_split, g * QPG + (i + 1))
                        src, buf, _, _ = quarter(i + NRAW)
                        sp.dma_start(buf, src).then_inc(raw_in[(i + NRAW) % NRAW], 16)
                sp.wait_ge(w_split, NG * QPG + 1)
                src, buf, _, _ = quarter(NRAW)
                sp.dma_start(buf, src).then_inc(raw_in[0], 16)

            @block.tensor
            def _(pe):
                readers = {PK: (head_normed, 13, 0), PVA: (va_done, 5, 0), PQ: (head_normed, 13, 5),
                           PQ + 1: (head_normed, 13, 9), PGB: (tanh_b, KT, 0), PGB + 1: (tanh_b, KT, 4),
                           PPB: (mb_done, KT, 0), PPB + 1: (mb_done, KT, 4), PV: (gelu_v, 8, 0), PV + 1: (gelu_v, 8, 4),
                           PU: (uT_ready, KT, 0), PU + 1: (uT_ready, KT, 4), PGA: (tanh_a, KT, 0),
                           PGA + 1: (tanh_a, KT, 4), PPA: (ya_gated, KT, 0), PPA + 1: (ya_gated, KT, 4),
                           POUT: (x2_done, 8, 8), POUT + 1: (x2_done, 8, 12)}
                last = [None] * 4

                def take(b, g, reader, per, n):
                    if last[b] is not None:
                        sem_, per_, n_ = last[b]
                        pe.wait_ge(sem_, g * per_ + n_)
                    last[b] = (reader, per, n)
                    return aux[b]

                def transpose_h(g, k, ahead):
                    bank = take(k % 4, g, hT_done, KT, ahead * KT + k + 1)
                    for t in range(GT):
                        mm = pe.transpose(bank[:, t * P:(t + 1) * P], xn[:, t, k * P:(k + 1) * P], ident)
                    mm.then_inc(hT_ps, 1)

                def transpose_halo(g, ahead):
                    for b in range(2):
                        bank = take(b, g, hx_done, 2, 2 * ahead + b + 1)
                        for k in range(4):
                            c = (4 * b + k) * P
                            mm = pe.transpose(bank[:, k * P:(k + 1) * P], xh[:, c:c + P], ident)
                        mm.then_inc(hx_ps, 1)

                pe.wait_ge(ws_in, 16)
                pe.wait_ge(const_in, 96)
                for b in range(2):
                    for k in range(4):
                        mm = pe.transpose(aux[b][:, k * P:(k + 1) * P],
                                          ws[:, 4 * b + k, :], ident)
                    mm.then_inc(ws_ps, 1)
                    last[b] = (ws_done, 0, b + 1)
                pe.wait_ge(xn_ready, 5)
                for k in range(KT):
                    transpose_h(0, k, 0)
                transpose_halo(0, 0)

                def token_major(bank, stat_hi, stat_lo, p, side=None):
                    n = PANELS[p][2]
                    hi, lo = w_hi[p % 2], w_lo[p % 2]
                    for k in range(KT):
                        pe.matmul(bank[:, 0:n], stat_hi(k), hi[:, k, 0:n], start=(k == 0), stop=False)
                        pe.matmul(bank[:, 0:n], stat_hi(k), lo[:, k, 0:n], start=False, stop=False)
                        mm = pe.matmul(bank[:, 0:n], stat_lo(k), hi[:, k, 0:n], start=False, stop=(k == KT - 1))
                    return mm

                def feature_major(bank, mov_hi, mov_lo, p, j, side=None):
                    hi, lo = w_hi[p % 2][:, :, j * P:(j + 1) * P], w_lo[p % 2][:, :, j * P:(j + 1) * P]
                    for k in range(KT):
                        pe.matmul(bank[:], hi[:, k, :], mov_hi[:, k, :], start=(k == 0), stop=False)
                        pe.matmul(bank[:], hi[:, k, :], mov_lo[:, k, :], start=False, stop=False)
                        mm = pe.matmul(bank[:], lo[:, k, :], mov_hi[:, k, :], start=False, stop=(k == KT - 1))
                        if side is not None and k % 2:
                            side(k // 2)
                    return mm

                def kT_tile(g, t):
                    pe.wait_ge(head_roped, g * 13 + (t + 1))
                    bank = take(2 + t % 2, g, kT_done, 5, t + 1)
                    for h in range(NKV):
                        mm = pe.transpose(bank[:, h * P:(h + 1) * P], kn[:, t, h * P:(h + 1) * P], ident)
                    mm.then_inc(kT_ps, 1)

                def qT_tile(g, i):
                    pe.wait_ge(head_roped, g * 13 + (5 + i + 1))
                    bank = take(2 + i % 2, g, qT_done, 8, i + 1)
                    for h in range(4):
                        mm = pe.transpose(bank[:, h * P:(h + 1) * P], qn[:, i // GT, i % GT, h * P:(h + 1) * P], ident)
                    mm.then_inc(qT_ps, 1)

                def attend(g, s):
                    if s < NU:
                        h, n = divmod(s, GT)
                        if s == 0:
                            pe.wait_ge(kT_done, g * 5 + 5)
                            pe.wait_ge(va_done, g * 5 + 5)
                            pe.wait_ge(halo_kept, g + 1)
                        if s % 16 == 0:
                            pe.wait_ge(qT_done, g * 8 + (s // 4 + 4))
                        bank = take(s % 2, g, s_masked, NU, s + 1)
                        pe.matmul(bank[:, 0:3 * P], qT[:, h, n * P:(n + 1) * P],
                                  kT[:, h // REP, n * P:(n + 3) * P], start=True, stop=True).then_inc(s_ps, 1)
                    if 0 <= s - 2 < NU:
                        u = s - 2
                        pe.wait_ge(p_ready, g * NU + (u + 1))
                        bank = take(2, g, pt_ready, NU, u + 1)
                        for c in range(3):
                            mm = pe.transpose(bank[:, c * P:(c + 1) * P], pr[u % 3][:, c * P:(c + 1) * P], ident)
                        mm.then_inc(pt_ps, 1)
                    if 0 <= s - 3 < NU:
                        u = s - 3
                        h, n = divmod(u, GT)
                        pe.wait_ge(pt_ready, g * NU + (u + 1))
                        bank = take(3, g, o_done, NU, u + 1)
                        for c in range(3):
                            v = va[:, n + c, (h // REP) * HD:(h // REP + 1) * HD]
                            mm = pe.matmul(bank[:, 0:P], v, pt[u % 2][:, c * P:(c + 1) * P], start=(c == 0), stop=(c == 2))
                        mm.then_inc(o_ps, 1)

                def spatial(g, c):
                    bank = take(c % 4, g, mixed_ready, KT, c + 1)
                    for n in range(GT):
                        mm = pe.matmul(bank[:, n * P:(n + 1) * P], vn[:, n, c * P:(c + 1) * P], wsT[:, c, :],
                                       start=True, stop=True)
                    mm.then_inc(sp_ps, 1)

                first = list(last)
                with pe.Fori(0, NG) as g:
                    for p in range(NP):
                        if p == PK:
                            pe.wait_ge(hT_done, g * KT + KT)
                        if p == PPB:
                            for s in range(NU, NU + 3):
                                attend(g, s)
                            pe.wait_ge(o_done, g * NU + NU)
                        if p == PPA:
                            pe.wait_ge(a_done, g * KT + KT)
                        if p == POUT:
                            pe.wait_ge(m_done, g * KT + KT)
                        if p == PU + 1:
                            pe.wait_ge(vn_ready, g * GT + GT)
                        if p == PGA:
                            for c in range(4, 8):
                                spatial(g, c)
                        if p == POUT + 1:
                            pe.wait_ge(xn_ready, g * 5 + 10)
                        pe.wait_ge(w_split, g * QPG + NQ * (p + 1))
                        for j in range(4):
                            side = None
                            if p in (PVA,):
                                kT_tile(g, j)
                            if p == PQ + 1:
                                qT_tile(g, j)
                            if p == PGB:
                                qT_tile(g, 4 + j)
                            if p == PU + 1:
                                spatial(g, j)
                            if p == POUT + 1:
                                transpose_h(g, 2 * j, 1)
                                transpose_h(g, 2 * j + 1, 1)
                                if j == 3:
                                    transpose_halo(g, 1)
                            if p in (PGB, PGB + 1):
                                def side(i, p=p, j=j):
                                    attend(g, 16 * (p - PGB) + 4 * j + i)
                            reader, per, n = readers[p - 1] if p else (x2_done, 8, 4)
                            pe.wait_ge(reader, g * per + (n + j + 1))
                            bank = main[j]
                            if p in (PK, PVA, PQ, PQ + 1, PV, PV + 1):
                                mm = token_major(bank, lambda k: hT_hi[:, k, j * P:(j + 1) * P],
                                                 lambda k: hT_lo[:, k, j * P:(j + 1) * P], p)
                            elif p >= POUT:
                                mm = token_major(bank, lambda k: m_hi[:, k, j * P:(j + 1) * P],
                                                 lambda k: m_lo[:, k, j * P:(j + 1) * P], p)
                            elif p in (PPB, PPB + 1):
                                mm = feature_major(bank, oT_hi, oT_lo, p, j)
                            elif p in (PPA, PPA + 1):
                                mm = feature_major(bank, aT_hi, aT_lo, p, j)
                            else:
                                mm = feature_major(bank, hT_hi, hT_lo, p, j, side)
                            mm.then_inc(out_ready, 1)
                        if p in (PK, PVA):
                            if p == PK:
                                pe.wait_ge(hx_done, g * 2 + 2)
                            bank = take(p, g, *((head_normed, 13, 5) if p == PK else (va_done, 5, 5)))
                            token_major(bank, lambda k: hx_hi[:, k, :], lambda k: hx_lo[:, k, :], p).then_inc(halo_ready, 1)
                        if p == PVA:
                            kT_tile(g, 4)

            @block.scalar
            def _(act):
                def split_hi(g, i):
                    _, buf, hi, _ = quarter(i)
                    act.wait_ge(raw_in[i % NRAW], (g * (QPG // NRAW) + (i // NRAW + 1)) * 16)
                    p = i // NQ - 2
                    if p in (PK, PVA):
                        act.wait_ge(halo_ready, g * 2 + (p + 1))
                    elif p > PVA:
                        act.wait_ge(out_ready, g * 4 * NP + 4 * (p + 1))
                    act.activation(hi, buf, ACT.Copy).then_inc(w_hi_done, 1)

                def prep(n, k):
                    if k < 0:
                        act.wait_ge(x_in, n * 16 + 16)
                        for t in range(GT):
                            if t:
                                act.wait_ge(ssx_ready, n * 5 + t)
                            act.activation(junk, xn[:, t, :], ACT.Square, accum_out=ssx[:, t:t + 1]).then_inc(ssx_ready, 1)
                        act.wait_ge(xh_in, n * 16 + 16)
                        act.wait_ge(ssx_ready, n * 5 + 4)
                        act.activation(junk, xh, ACT.Square, accum_out=ssx[:, 4:5]).then_inc(ssx_ready, 1)
                    elif k < KT:
                        act.wait_ge(hT_ps, n * KT + (k + 1))
                        act.activation(hT_hi[:, k, :], aux[k % 4][:], ACT.Copy, scale=g_mix[:, k:k + 1]).then_inc(hT_hi_done, 1)
                    else:
                        b = k - KT
                        act.wait_ge(hx_ps, n * 2 + (b + 1))
                        for i in range(4):
                            ins = act.activation(hx_hi[:, 4 * b + i, :], aux[b][:, i * P:(i + 1) * P], ACT.Copy,
                                                 scale=g_mix[:, 4 * b + i:4 * b + i + 1])
                        ins.then_inc(hx_hi_done, 1)

                act.wait_ge(const_in, 96)
                for b in range(2):
                    act.wait_ge(ws_ps, b + 1)
                    act.activation(wsT[:, 4 * b:4 * b + 4, :], aux[b][:].rearrange("p (k q) -> p k q", k=4),
                                   ACT.Copy).then_inc(ws_done, 1)
                act.activation(nsink, sink, ACT.Copy, scale=-1.0)
                for i in range(NQ):
                    split_hi(0, i)
                for k in range(-1, KT + 2):
                    prep(0, k)

                def attend(g, s):
                    if 0 <= s - 2 < NU:
                        u = s - 2
                        act.wait_ge(pt_ps, g * NU + (u + 1))
                        if u >= 2:
                            act.wait_ge(o_ps, g * NU + (u - 1))
                        ins = act.activation(pt[u % 2], aux[2][:, 0:3 * P], ACT.Copy)
                        ins.then_inc(pt_ready, 1)
                    if s < NU:
                        h = s // GT
                        act.wait_ge(negm_ready, g * NU + (s + 1))
                        if s >= 3:
                            act.wait_ge(pt_ps, g * NU + (s - 2))
                        act.activation(pr[s % 3], sm[s % 2], ACT.Exp, bias=stat[:, s % 4, 1:2], scale=SCALE,
                                       accum_out=stat[:, s % 4, 2:3])
                        act.activation(stat[:, s % 4, 3:4], stat[:, s % 4, 1:2], ACT.Exp,
                                       bias=sink[:, h:h + 1]).then_inc(exp_done, 1)
                    if 0 <= s - 3 < NU:
                        u = s - 3
                        h, n = divmod(u, GT)
                        act.wait_ge(o_ps, g * NU + (u + 1))
                        act.activation(oT_hi[:, h, n * P:(n + 1) * P], aux[3][:, 0:P], ACT.Copy).then_inc(o_hi_done, 1)

                def copy_kT(g, t):
                    act.wait_ge(kT_ps, g * 5 + (t + 1))
                    b = 2 + t % 2
                    act.activation(kT[:, :, (t + 1) * P:(t + 2) * P], aux[b][:, 0:2 * P].rearrange("p (h q) -> p h q", h=2),
                                   ACT.Copy).then_inc(kT_done, 1)

                def copy_qT(g, i):
                    act.wait_ge(qT_ps, g * 8 + (i + 1))
                    b, q, t = 2 + i % 2, i // GT, i % GT
                    act.activation(qT[:, 4 * q:4 * q + 4, t * P:(t + 1) * P], aux[b][:].rearrange("p (h q) -> p h q", h=4),
                                   ACT.Copy).then_inc(qT_done, 1)

                def round_a(g, c):
                    act.wait_ge(a_ready, g * KT + (c + 1))
                    act.activation(aT_hi[:, c, :], tmp[c % 2], ACT.Copy).then_inc(a_hi_done, 1)

                def round_m(g, c):
                    act.wait_ge(m_ready, g * KT + (c + 1))
                    act.activation(m_hi[:, c, :], tmp[c % 2], ACT.Copy).then_inc(m_hi_done, 1)

                with act.Fori(0, NG) as g:
                    for p in range(NP):
                        if p == PPB:
                            for s in range(NU, NU + 3):
                                attend(g, s)
                        for j in range(4):
                            split_hi(g, NQ * (p + 1) + j)
                            if p == POUT and j == 2:
                                prep(g + 1, -1)
                            o = g * 4 * NP + (4 * p + j + 1)
                            if p == PVA:
                                copy_kT(g, j)
                            if p == PQ + 1:
                                copy_qT(g, j)
                            if p == PGB:
                                copy_qT(g, 4 + j)
                            if p in (PGB, PGB + 1):
                                for i in range(4):
                                    attend(g, 16 * (p - PGB) + 4 * j + i)
                            if p == PGA:
                                round_a(g, 4 + j)
                            if p == PU + 1:
                                round_a(g, j)
                            if p == POUT + 1:
                                prep(g + 1, 2 * j)
                                prep(g + 1, 2 * j + 1)
                                if j == 3:
                                    prep(g + 1, KT)
                                    prep(g + 1, KT + 1)
                            if p in (PK, PQ, PQ + 1):
                                n = 256 if p == PK else 512
                                i = j if p == PK else 5 + 4 * (p - PQ) + j
                                act.wait_ge(out_ready, o)
                                if i:
                                    act.wait_ge(ssq_ready, g * 13 + i)
                                act.activation(sq[:, 0:n], main[j][:, 0:n], ACT.Square).then_inc(sq_ready, 1)
                            if p == PVA:
                                act.wait_ge(out_ready, o)
                                act.activation(va[:, j + 1, :], main[j][:, 0:256], ACT.Copy).then_inc(va_done, 1)
                            if p in (PGB, PGB + 1):
                                act.wait_ge(out_ready, o)
                                act.activation(sgb[:, 4 * (p - PGB) + j, :], main[j][:], ACT.Tanh, scale=0.5).then_inc(tanh_b, 1)
                            if p in (PV, PV + 1):
                                q = p - PV
                                act.wait_ge(out_ready, o)
                                v = vn[:, j, q * 512:(q + 1) * 512]
                                act.activation(v, main[j][:], ACT.Gelu_apprx_tanh).then_inc(gelu_v, 1)
                                act.wait_ge(gelu_v, g * 8 + (4 * q + j + 1))
                                if q or j:
                                    act.wait_ge(ssv_ready, g * 8 + (4 * q + j))
                                act.activation(junk[:, 0:512], v, ACT.Square, accum_out=ssv[:, j, q:q + 1]).then_inc(ssv_ready, 1)
                            if p in (PU, PU + 1):
                                c = 4 * (p - PU) + j
                                act.wait_ge(out_ready, o)
                                act.activation(uT[:, c, :], main[j][:], ACT.Gelu_apprx_tanh).then_inc(uT_ready, 1)
                            if p in (PGA, PGA + 1):
                                c = 4 * (p - PGA) + j
                                act.wait_ge(out_ready, o)
                                act.activation(sga[:, c, :], main[j][:], ACT.Tanh, scale=0.5).then_inc(tanh_a, 1)
                            if p in (PPA, PPA + 1):
                                round_m(g, 4 * (p - PPA) + j)
                        if p == PK:
                            act.wait_ge(halo_ready, g * 2 + 1)
                            act.wait_ge(ssq_ready, g * 13 + 4)
                            act.activation(sq[:, 0:256], aux[0][:, 0:256], ACT.Square).then_inc(sq_ready, 1)
                        if p == PVA:
                            act.wait_ge(halo_ready, g * 2 + 2)
                            act.activation(va[:, 5, :], aux[1][:, 0:256], ACT.Copy).then_inc(va_done, 1)
                            copy_kT(g, 4)
                    act.wait_ge(out_ready, g * 4 * NP + 4 * NP)

            @block.vector
            def _(dve):
                def split_lo(g, i):
                    _, buf, hi, lo = quarter(i)
                    dve.wait_ge(w_hi_done, g * QPG + (i + 1))
                    dve.tensor_tensor(lo, buf, hi.bitcast(F32), ALU.subtract).then_inc(w_split, 1)

                def prep(n, k):
                    if k < 0:
                        dve.wait_ge(rsx_ready, n + 1)
                        for t in range(GT):
                            dve.tensor_scalar(xn[:, t, :], xn[:, t, :], rsx[:, t:t + 1], None, ALU.mult).then_inc(xn_ready, 1)
                        dve.tensor_scalar(xh, xh, rsx[:, 4:5], None, ALU.mult).then_inc(xn_ready, 1)
                    elif k < KT:
                        dve.wait_ge(hT_hi_done, n * KT + (k + 1))
                        dve.scalar_tensor_tensor(out=hT_lo[:, k, :], in0=aux[k % 4][:], scalar=g_mix[:, k:k + 1],
                                                 in1=hT_hi[:, k, :].bitcast(F32), op0=ALU.mult,
                                                 op1=ALU.subtract).then_inc(hT_done, 1)
                    else:
                        b = k - KT
                        dve.wait_ge(hx_hi_done, n * 2 + (b + 1))
                        for i in range(4):
                            ins = dve.scalar_tensor_tensor(
                                out=hx_lo[:, 4 * b + i, :], in0=aux[b][:, i * P:(i + 1) * P],
                                scalar=g_mix[:, 4 * b + i:4 * b + i + 1], in1=hx_hi[:, 4 * b + i, :].bitcast(F32),
                                op0=ALU.mult, op1=ALU.subtract)
                        ins.then_inc(hx_done, 1)

                dve.sem_inc(x2_done, 8)
                dve.memset(kT[:, :, 0:P], 0.0)
                dve.memset(va[:, 0, :], 0.0).then_inc(halo_kept, 1)
                for i in range(NQ):
                    split_lo(0, i)
                dve.wait_ge(const_in, 96)
                for k in range(-1, KT + 2):
                    prep(0, k)

                def head_norm(g, i, bank, n, dst):
                    h = n // HD
                    dve.wait_ge(sq_ready, g * 13 + (i + 1))
                    dve.reduce_sum(ssq[:, 0:h], sq[:, 0:n].rearrange("p (h d) -> p h d", h=h), AX_X).then_inc(ssq_ready, 1)
                    dve.wait_ge(rsq_ready, g * 13 + (i + 1))
                    dve.tensor_tensor(dst, bank[:, 0:n].rearrange("p (h d) -> p h d", h=h),
                                      rsq[:, 0:h].unsqueeze(2).to_broadcast([P, h, HD]), ALU.mult).then_inc(head_normed, 1)

                def attend(g, s):
                    if s < NU:
                        n, b = s % GT, s % 2
                        m = 0 if n == 0 else 2 if n == GT - 1 else 1
                        st = stat[:, s % 4, :]
                        dve.wait_ge(s_ps, g * NU + (s + 1))
                        if s == 0:
                            dve.wait_ge(table_in, g * 32 + 32)
                        if s >= 2:
                            dve.wait_ge(exp_done, g * NU + (s - 1))
                        dve.sem_inc(settled, 1)
                        dve.tensor_tensor_reduce(sm[b], aux[b][:, 0:3 * P], mask[:, m, :], 1.0, -BIG, ALU.add, ALU.max,
                                                 st[:, 0:1]).then_inc(s_masked, 1)
                        dve.wait_ge(s_masked, g * NU + (s + 1))
                        dve.tensor_scalar(st[:, 1:2], st[:, 0:1], -SCALE, nsink[:, s // GT:s // GT + 1],
                                          ALU.mult, ALU.min).then_inc(negm_ready, 1)
                    if 0 <= s - 1 < NU:
                        u = s - 1
                        st = stat[:, u % 4, :]
                        dve.wait_ge(exp_done, g * NU + (u + 1))
                        dve.tensor_tensor(st[:, 4:5], st[:, 2:3], st[:, 3:4], ALU.add).then_inc(dve_step, 1)
                        dve.wait_ge(dve_step, g * NU + (u + 1))
                        dve.reciprocal(st[:, 5:6], st[:, 4:5]).then_inc(rden_ready, 1)
                    if 0 <= s - 3 < NU:
                        u = s - 3
                        h, n = divmod(u, GT)
                        dve.wait_ge(o_hi_done, g * NU + (u + 1))
                        dve.tensor_tensor(oT_lo[:, h, n * P:(n + 1) * P], aux[3][:, 0:P],
                                          oT_hi[:, h, n * P:(n + 1) * P].bitcast(F32), ALU.subtract).then_inc(o_done, 1)

                def mixed(g, c):
                    dve.wait_ge(sp_ps, g * KT + (c + 1))
                    if c == 0:
                        dve.wait_ge(bsp_in, g * 16 + 16)
                    if c >= 2:
                        dve.wait_ge(a_done, g * KT + (c - 1))
                    dve.scalar_tensor_tensor(out=tmp[c % 2].rearrange("p (n q) -> p n q", n=GT),
                                             in0=aux[c % 4][:].rearrange("p (n q) -> p n q", n=GT),
                                             scalar=g_v[:, c:c + 1],
                                             in1=bsp[:, c, :].unsqueeze(1).to_broadcast([P, GT, P]),
                                             op0=ALU.mult, op1=ALU.add).then_inc(mixed_ready, 1)

                def a_lo(g, c):
                    dve.wait_ge(a_hi_done, g * KT + (c + 1))
                    dve.tensor_tensor(aT_lo[:, c, :], tmp[c % 2], aT_hi[:, c, :].bitcast(F32),
                                      ALU.subtract).then_inc(a_done, 1)

                with dve.Fori(0, NG) as g:
                    for p in range(NP):
                        if p == PPB:
                            for s in range(NU, NU + 3):
                                attend(g, s)
                        if p == PU:
                            dve.wait_ge(rsv_ready, g + 1)
                            for t in range(GT):
                                dve.tensor_scalar(vn[:, t, :], vn[:, t, :], rsv[:, t:t + 1], None, ALU.mult).then_inc(vn_ready, 1)
                        for j in range(4):
                            split_lo(g, NQ * (p + 1) + j)
                            if p == POUT and j == 2:
                                prep(g + 1, -1)
                            o = g * 4 * NP + (4 * p + j + 1)
                            if p in (PGB, PGB + 1):
                                for i in range(4):
                                    attend(g, 16 * (p - PGB) + 4 * j + i)
                            if p == PU + 1:
                                mixed(g, j)
                                a_lo(g, j)
                            if p == PGA:
                                mixed(g, 4 + j)
                                a_lo(g, 4 + j)
                            if p == POUT + 1:
                                prep(g + 1, 2 * j)
                                prep(g + 1, 2 * j + 1)
                                if j == 3:
                                    prep(g + 1, KT)
                                    prep(g + 1, KT + 1)
                            if p == PK:
                                head_norm(g, j, main[j], 256, kn[:, j, :].rearrange("p (h d) -> p h d", h=2))
                            if p in (PQ, PQ + 1):
                                head_norm(g, 5 + 4 * (p - PQ) + j, main[j], 512,
                                          qn[:, p - PQ, j, :].rearrange("p (h d) -> p h d", h=4))
                            if p in (PPB, PPB + 1):
                                c = 4 * (p - PPB) + j
                                dve.wait_ge(out_ready, o)
                                dve.wait_ge(sgb_ready, g * KT + (c + 1))
                                dve.tensor_tensor(sgb[:, c, :], main[j][:], sgb[:, c, :], ALU.mult).then_inc(mb_done, 1)
                            if p in (PPA, PPA + 1):
                                c = 4 * (p - PPA) + j
                                dve.wait_ge(out_ready, o)
                                dve.wait_ge(sga_ready, g * KT + (c + 1))
                                if c >= 2:
                                    dve.wait_ge(m_done, g * KT + (c - 1))
                                dve.tensor_tensor(tmp[c % 2], main[j][:], sga[:, c, :], ALU.mult).then_inc(ya_gated, 1)
                                dve.wait_ge(m_hi_done, g * KT + (c + 1))
                                dve.tensor_tensor(m_lo[:, c, :], tmp[c % 2], m_hi[:, c, :].bitcast(F32),
                                                  ALU.subtract).then_inc(m_done, 1)
                            if p >= POUT:
                                q = p - POUT
                                dve.wait_ge(out_ready, o)
                                if q == 0 and j == 0:
                                    dve.wait_ge(x2_in, g * 16 + 16)
                                r = x2[:, j, q * 512:(q + 1) * 512]
                                dve.tensor_tensor(r, main[j][:], r, ALU.add).then_inc(x2_done, 1)
                        if p == PK:
                            head_norm(g, 4, aux[0], 256, kn[:, 4, :].rearrange("p (h d) -> p h d", h=2))

            @block.gpsimd
            def _(pool):
                def settle():
                    pool.sem_inc(settled, 1)

                def rms(out, ss, n, width, link):
                    settle()
                    pool.tensor_scalar(out, ss, 1.0 / width, EPS, ALU.mult, ALU.add).then_inc(pool_step, 1)
                    pool.wait_ge(pool_step, link())
                    return pool.tensor_tensor(out, out, half[:, 0:n], ALU.pow)

                counted = {"n": 0, "per": 0}

                def link_at(g, base):
                    def link():
                        counted["n"] += 1
                        return g * PER_BODY + (base + counted["n"])
                    return link

                PREP_STEPS = 1
                PER_BODY = 13 * 4 + 2 + 1

                def load_group(n, row, halo):
                    pool.dma_start(xn, a["x_all"][bass.ds(row, G), :].rearrange("(t p) d -> p t d", p=P)).then_inc(x_in, 16)
                    pool.dma_start(xh, a["x_all"][bass.ds(halo, P), :]).then_inc(xh_in, 16)
                    pool.dma_start(rope, a["rope"][bass.ds(n * P, P), :].rearrange("p (t c f) -> p t c f", t=5, c=2)).then_inc(table_in, 16)
                    pool.dma_start(mask, a["mask"][bass.ds(n * P, P), :].rearrange("p (m k) -> p m k", m=3)).then_inc(table_in, 16)

                pool.dma_start(ws, a["w_spatial"].rearrange("g p q -> p g q")).then_inc(ws_in, 16)
                pool.memset(half, -0.5).then_inc(const_set, 1)
                pool.wait_ge(const_set, 1)
                load_group(0, 0, G)
                pool.wait_ge(ssx_ready, 5)
                rms(rsx[:, 0:5], ssx[:, 0:5], 5, D, link_at(0, 0)).then_inc(rsx_ready, 1)
                counted["n"] = 0
                pool.wait_ge(const_in, 96)

                with pool.Fori(0, NG) as g:
                    link = link_at(g, PREP_STEPS)

                    def rope_heads(i, t, n, gain, dst):
                        h = n // HD
                        pool.wait_ge(ssq_ready, g * 13 + (i + 1))
                        rms(rsq[:, 0:h], ssq[:, 0:h], h, HD, link).then_inc(rsq_ready, 1)
                        pool.wait_ge(head_normed, g * 13 + (i + 1))
                        x = dst.rearrange("p (h d) -> p h d", h=h)
                        pool.tensor_tensor(x, x, gain.unsqueeze(1).to_broadcast([P, h, HD]), ALU.mult).then_inc(pool_step, 1)
                        pool.wait_ge(pool_step, link())
                        r = rot[:, 0:n].rearrange("p (h d) -> p h d", h=h)
                        hf = HD // 2
                        cos = rope[:, t, 0, :].unsqueeze(1).to_broadcast([P, h, hf])
                        sin = rope[:, t, 1, :].unsqueeze(1).to_broadcast([P, h, hf])
                        x1, x2_ = x[:, :, 0:hf], x[:, :, hf:HD]
                        pool.tensor_tensor(r[:, :, 0:hf], x2_, sin, ALU.mult)
                        pool.tensor_tensor(r[:, :, hf:HD], x1, sin, ALU.mult).then_inc(pool_step, 1)
                        pool.wait_ge(pool_step, link())
                        pool.tensor_tensor(x1, x1, cos, ALU.mult)
                        pool.tensor_tensor(x2_, x2_, cos, ALU.mult).then_inc(pool_step, 1)
                        pool.wait_ge(pool_step, link())
                        pool.tensor_tensor(x1, x1, r[:, :, 0:hf], ALU.subtract)
                        pool.tensor_tensor(x2_, x2_, r[:, :, hf:HD], ALU.add).then_inc(head_roped, 1)
                        pool.wait_ge(head_roped, g * 13 + (i + 1))

                    def weigh(s):
                        if 0 <= s < NU:
                            pool.wait_ge(rden_ready, g * NU + (s + 1))
                            settle()
                            pool.tensor_scalar(pr[s % 3], pr[s % 3], stat[:, s % 4, 5:6], 1.0, ALU.mult,
                                               ALU.mult).then_inc(p_ready, 1)

                    pool.wait_ge(table_in, g * 32 + 32)
                    for t in range(5):
                        rope_heads(t, t, 256, gk, kn[:, t, :])
                    for i in range(8):
                        rope_heads(5 + i, i % GT, 512, gq, qn[:, i // GT, i % GT, :])
                    for c in range(KT):
                        for s in range(4 * c, 4 * c + 4):
                            weigh(s - 1)
                        pool.wait_ge(tanh_b, g * KT + (c + 1))
                        settle()
                        pool.tensor_scalar(sgb[:, c, :], sgb[:, c, :], 0.5, 0.5, ALU.mult, ALU.add).then_inc(sgb_ready, 1)
                    weigh(NU - 1)
                    pool.wait_ge(o_ps, g * NU + NU)
                    settle()
                    pool.tensor_copy(kT[:, :, 0:P], kT[:, :, GT * P:(GT + 1) * P])
                    pool.tensor_copy(va[:, 0, :], va[:, GT, :]).then_inc(halo_kept, 1)
                    pool.dma_start(bsp, a["b_spatial"].to_broadcast([P, NH * P]).rearrange("p (g q) -> p g q", g=NH)).then_inc(bsp_in, 16)
                    pool.wait_ge(ssv_ready, g * 8 + 8)
                    pool.tensor_tensor(rsv, ssv[:, :, 0], ssv[:, :, 1], ALU.add).then_inc(pool_step, 1)
                    pool.wait_ge(pool_step, link())
                    rms(rsv, rsv, GT, D, link).then_inc(rsv_ready, 1)
                    for c in range(KT):
                        pool.wait_ge(mixed_ready, g * KT + (c + 1))
                        pool.wait_ge(uT_ready, g * KT + (c + 1))
                        pool.tensor_tensor(tmp[c % 2], tmp[c % 2], uT[:, c, :], ALU.mult).then_inc(a_ready, 1)
                        if c >= 4:
                            pool.wait_ge(tanh_a, g * KT + (c - 3))
                            settle()
                            pool.tensor_scalar(sga[:, c - 4, :], sga[:, c - 4, :], 0.5, 0.5, ALU.mult, ALU.add).then_inc(sga_ready, 1)
                    for c in range(4, KT):
                        pool.wait_ge(tanh_a, g * KT + (c + 1))
                        settle()
                        pool.tensor_scalar(sga[:, c, :], sga[:, c, :], 0.5, 0.5, ALU.mult, ALU.add).then_inc(sga_ready, 1)
                    for c in range(KT):
                        pool.wait_ge(ya_gated, g * KT + (c + 1))
                        pool.tensor_tensor(tmp[c % 2], tmp[c % 2], sgb[:, c, :], ALU.add).then_inc(m_ready, 1)
                    pool.wait_ge(out_ready, g * 4 * NP + 4 * (PPA + 2))
                    pool.wait_ge(m_done, g * KT + KT)
                    settle()
                    pool.dma_start(x2, a["x_all"][bass.ds(g * G, G), :].rearrange("(t p) d -> p t d", p=P)).then_inc(x2_in, 16)
                    load_group(g + 1, g * G + G, g * G + 2 * G)
                    pool.wait_ge(ssx_ready, g * 5 + 10)
                    rms(rsx[:, 0:5], ssx[:, 0:5], 5, D, link).then_inc(rsx_ready, 1)
                    for t in range(GT):
                        pool.wait_ge(x2_done, g * 8 + (8 + 4 + t + 1))
                        settle()
                        for dst in (a["y"], a["x2s"]):
                            pool.dma_start(dst[bass.ds(g * G + t * P, P), :], x2[:, t, :]).then_inc(y_out, 16)
                    pool.wait_ge(y_out, g * 2 * GT * 16 + 2 * GT * 16)
                assert counted["n"] == PER_BODY, counted


def route(nc, a):
    with ExitStack() as ctx:
        def sb(name, shape, dt=F32):
            return ctx.enter_context(nc.sbuf_tensor(name, shape, dt))[...]

        def sem(name):
            return ctx.enter_context(nc.semaphore(name))

        x = sb("r_x", [P, NT, D])
        junk = sb("r_junk", [P, D])
        h2T = sb("r_h2T", [P, 2, KT, G])
        w_r = sb("r_w", [P, KT, N_GROUPS + NE])
        bias = sb("r_bias", [P, N_GROUPS + NE])
        g_ffn = sb("r_g", [P, KT])
        ident, upper, ones = sb("r_ident", [P, P]), sb("r_upper", [P, P]), sb("r_ones", [P, P])
        cst = sb("r_cst", [P, 2, EPG + NE])
        ids = sb("r_ids", [P, NT], I32)
        pad = sb("r_pad", [P, CAP * NE // P, 2])
        zero = sb("r_zero", [P, D])
        half = sb("r_half", [P, NT])
        ss, rs = sb("r_ss", [P, NT]), sb("r_rs", [P, NT])
        logits = sb("r_logits", [P, NT, N_GROUPS + NE])
        gmax, gsum, gp = sb("r_gmax", [P, NT]), sb("r_gsum", [P, NT]), sb("r_gp", [P, NT])
        s4, eg, ohg = sb("r_s4", [P, NT, N_GROUPS]), sb("r_eg", [P, NT, N_GROUPS]), sb("r_ohg", [P, NT, N_GROUPS])
        pick = sb("r_pick", [P, NT])
        prod = sb("r_prod", [P, NT, NE])
        esel, s8 = sb("r_esel", [P, NT, EPG]), sb("r_s8", [P, NT, EPG])
        oh = [sb(f"r_oh{k}", [P, NT, EPG]) for k in range(2)]
        m = [sb(f"r_m{k}", [P, NT]) for k in range(2)]
        dif, ratio, den = sb("r_dif", [P, NT]), sb("r_ratio", [P, NT]), sb("r_den", [P, NT])
        A = [sb(f"r_A{k}", [P, NT, NE]) for k in range(2)]
        Asum = sb("r_Asum", [P, NT, NE])
        cum = sb("r_cum", [P, NT + 1, NE])
        pos = sb("r_pos", [P, NT, NE])
        dest_f, dest = sb("r_dest_f", [P, 2, NT]), sb("r_dest", [P, 2, NT], I32)
        ent = sb("r_ent", [P, 2, NT, 2])
        nb_i, nb = sb("r_nb_i", [1, NE], I32), sb("r_nb", [1, NE])
        pend = sb("r_pend", [1, NE])
        onesr = sb("r_onesr", [1, NE])
        bi = sb("r_bi", [1, NTAB])
        cmp_, cmpe = sb("r_cmp", [1, NTAB, NE]), sb("r_cmpe", [1, NTAB, NE])
        be, bs, bb = sb("r_be", [1, NTAB]), sb("r_bs", [1, NTAB]), sb("r_bb", [1, NTAB])
        new = sb("r_new", [1, NTAB])
        tab = sb("r_tab", [1, 4, NTAB], I32)

        bank = [ctx.enter_context(nc.psum_tensor(f"r_ps{i}", [P, 512], F32)) for i in range(8)]
        const_in, x_in, zero_set, set_done, ids_done, pads_out, slots_set = (
            sem("r_const_in"), [sem(f"r_x_in{i}") for i in range(NG)], sem("r_zero_set"), sem("r_set_done"),
            sem("r_ids_done"), sem("r_pads_out"), sem("r_slots_set"))
        sq_done, rs_done, t_ps, t_done, l_ps, l_done = (
            sem("r_sq_done"), sem("r_rs_done"), sem("r_t_ps"), sem("r_t_done"), sem("r_l_ps"), sem("r_l_done"))
        gsub_ready, eg_done, dif_ready, ratio_done, A_ready, rank_ps = (
            sem("r_gsub_ready"), sem("r_eg_done"), sem("r_dif_ready"), sem("r_ratio_done"), sem("r_A_ready"), sem("r_rank_ps"))
        step, pstep, ent_ready, tab_ready, list_out, tab_out = (
            sem("r_step"), sem("r_pstep"), sem("r_ent_ready"), sem("r_tab_ready"), sem("r_list_out"), sem("r_tab_out"))

        with nc.Block() as block:

            @block.sync
            def _(sp):
                for dst, name in ((ident, "ident"), (g_ffn, "norm_ffn_g"), (upper, "upper")):
                    sp.dma_start(dst, a[name]).then_inc(const_in, 16)
                sp.dma_start(w_r[:, :, 0:N_GROUPS], a["w_router_group"].rearrange("(k p) c -> p k c", p=P)).then_inc(const_in, 16)
                sp.dma_start(w_r[:, :, N_GROUPS:], a["w_router_expert"].rearrange("(k p) c -> p k c", p=P)).then_inc(const_in, 16)
                sp.dma_start(bias[:, 0:N_GROUPS], a["b_router_group"].to_broadcast([P, N_GROUPS])).then_inc(const_in, 16)
                sp.dma_start(bias[:, N_GROUPS:], a["b_router_expert"].to_broadcast([P, NE])).then_inc(const_in, 16)
                sp.dma_start(cst, a["counts"].to_broadcast([P, 2 * (EPG + NE)]).rearrange("p (a b) -> p a b", a=2)).then_inc(const_in, 16)
                sp.dma_start(bi, a["blocks"]).then_inc(const_in, 16)
                for r in range(NG):
                    sp.dma_start(x[:, r * GT:(r + 1) * GT, :],
                                 a["x2s"][r * G:(r + 1) * G, :].rearrange("(t p) d -> p t d", p=P)).then_inc(x_in[r], 16)
                sp.wait_ge(zero_set, 1)
                for dst in (a["y"], a["x2s"]):
                    sp.dma_start(dst[T:T + P, :], zero).then_inc(pads_out, 16)
                sp.wait_ge(tab_ready, 1)
                sp.dma_start(a["table"], tab).then_inc(tab_out, 16)
                sp.wait_ge(tab_out, 16)
                sp.wait_ge(pads_out, 32)

            @block.tensor
            def _(pe):
                pe.wait_ge(const_in, 9 * 16)

                def transposes(r, k):
                    pe.wait_ge(x_in[r], 16)
                    n = r * KT + k
                    if n >= 4:
                        pe.wait_ge(t_done, n - 3)
                    for t in range(GT):
                        mm = pe.transpose(bank[n % 4][:, t * P:(t + 1) * P], x[:, r * GT + t, k * P:(k + 1) * P], ident)
                    mm.then_inc(t_ps, 1)

                def products(r):
                    pe.wait_ge(t_done, (r + 1) * KT)
                    for t in range(GT):
                        for k in range(KT):
                            mm = pe.matmul(bank[4 + r][:, 64 * t:64 * t + N_GROUPS + NE], h2T[:, r % 2, k, t * P:(t + 1) * P],
                                           w_r[:, k, :], start=(k == 0), stop=(k == KT - 1))
                    mm.then_inc(l_ps, 1)

                for r in range(NG):
                    for k in range(KT):
                        transposes(r, k)
                    products(r)
                pe.wait_ge(A_ready, 1)
                pe.wait_ge(set_done, 1)
                flat = Asum.rearrange("p t e -> p (t e)")
                pe.matmul(bank[0][:, 0:NT * NE], upper, flat, start=True, stop=True)
                pe.matmul(bank[1][:, 0:NT * NE], ones, flat, start=True, stop=True).then_inc(rank_ps, 1)

            @block.scalar
            def _(act):
                act.wait_ge(const_in, 9 * 16)
                for r in range(NG):
                    act.wait_ge(x_in[r], 16)
                    for k in range(KT):
                        n = r * KT + k
                        act.wait_ge(t_ps, n + 1)
                        if r == 2 and k == 0:
                            act.wait_ge(l_ps, 1)
                        act.activation(h2T[:, r % 2, k, :], bank[n % 4][:], ACT.Copy, scale=g_ffn[:, k:k + 1]).then_inc(t_done, 1)
                        if k % 2:
                            t = r * GT + k // 2
                            if t:
                                act.wait_ge(sq_done, t)
                            act.activation(junk, x[:, t, :], ACT.Square, accum_out=ss[:, t:t + 1]).then_inc(sq_done, 1)
                act.wait_ge(gsub_ready, 1)
                act.activation(eg, s4, ACT.Exp).then_inc(eg_done, 1)
                act.wait_ge(dif_ready, 1)
                act.activation(ratio, dif, ACT.Exp).then_inc(ratio_done, 1)

            @block.vector
            def _(dve):
                n = [0]

                def link(ins):
                    n[0] += 1
                    ins.then_inc(step, 1)
                    dve.wait_ge(step, n[0])

                def over(ap, n_):
                    return ap.unsqueeze(2).to_broadcast([P, NT, n_])

                def across(ap):
                    return ap.unsqueeze(1).to_broadcast([P, NT, ap.shape[-1]])

                dve.memset(zero, 0.0).then_inc(zero_set, 1)
                dve.memset(onesr, 1.0)
                dve.memset(cum[:, 0, :], 0.0)
                dve.memset(ones, 1.0).then_inc(set_done, 1)
                dve.wait_ge(set_done, 1)
                dve.wait_ge(const_in, 9 * 16)
                dve.wait_ge(rs_done, 1)
                for r in range(NG):
                    dve.wait_ge(l_ps, r + 1)
                    for t in range(GT):
                        ins = dve.scalar_tensor_tensor(out=logits[:, r * GT + t, :], in0=bank[4 + r][:, 64 * t:64 * t + N_GROUPS + NE],
                                                       scalar=rs[:, r * GT + t:r * GT + t + 1], in1=bias, op0=ALU.mult, op1=ALU.add)
                link(ins)

                gl, el = logits[:, :, 0:N_GROUPS], logits[:, :, N_GROUPS:]

                def first_max(vals, width, top, scratch, onehot):
                    link(dve.tensor_reduce(top, vals, AX_X, ALU.max))
                    link(dve.tensor_tensor(scratch, vals, over(top, width), ALU.is_equal))
                    link(dve.scalar_tensor_tensor(out=scratch, in0=scratch, scalar=-100.0, in1=across(cst[:, 0, 0:width]),
                                                  op0=ALU.mult, op1=ALU.add))
                    link(dve.tensor_reduce(pick, scratch, AX_X, ALU.min))
                    link(dve.tensor_tensor(onehot, across(cst[:, 1, 0:width]), over(pick, width), ALU.is_equal))

                first_max(gl, N_GROUPS, gmax, s4, ohg)
                dve.tensor_tensor(s4, gl, over(gmax, N_GROUPS), ALU.subtract).then_inc(gsub_ready, 1)
                p4 = prod.rearrange("p t (g e) -> p t g e", g=N_GROUPS)
                link(dve.tensor_tensor(p4, el.rearrange("p t (g e) -> p t g e", g=N_GROUPS),
                                       ohg.unsqueeze(3).to_broadcast([P, NT, N_GROUPS, EPG]), ALU.mult))
                link(dve.reduce_sum(esel, prod.rearrange("p t (g e) -> p t e g", g=N_GROUPS), AX_X))
                first_max(esel, EPG, m[0], s8, oh[0])
                link(dve.scalar_tensor_tensor(out=esel, in0=oh[0], scalar=-BIG, in1=esel, op0=ALU.mult, op1=ALU.add))
                first_max(esel, EPG, m[1], s8, oh[1])
                dve.tensor_tensor(dif, m[1], m[0], ALU.subtract).then_inc(dif_ready, 1)
                for k in range(2):
                    link(dve.tensor_tensor(A[k].rearrange("p t (g e) -> p t g e", g=N_GROUPS),
                                           ohg.unsqueeze(3).to_broadcast([P, NT, N_GROUPS, EPG]),
                                           oh[k].unsqueeze(2).to_broadcast([P, NT, N_GROUPS, EPG]), ALU.mult))
                link(dve.tensor_tensor(Asum, A[0], A[1], ALU.add))
                dve.sem_inc(A_ready, 1)
                dve.wait_ge(eg_done, 1)
                link(dve.reduce_sum(gsum, eg, AX_X))
                link(dve.reciprocal(gp, gsum))
                dve.wait_ge(ratio_done, 1)
                link(dve.tensor_scalar(den, ratio, 1.0, None, ALU.add))
                link(dve.reciprocal(den, den))
                link(dve.tensor_tensor(ent[:, 0, :, 1], gp, den, ALU.mult))
                dve.wait_ge(ids_done, 1)
                for k in range(2):
                    dve.tensor_copy(ent[:, k, :, 0].bitcast(I32), ids)
                link(dve.tensor_tensor(ent[:, 1, :, 1], ent[:, 0, :, 1], ratio, ALU.mult))
                dve.wait_ge(rank_ps, 1)
                for t in range(NT):
                    link(dve.tensor_tensor(cum[:, t + 1, :], bank[1][:, t * NE:(t + 1) * NE], cum[:, t, :], ALU.add))
                link(dve.tensor_tensor(pos, bank[0][:, 0:NT * NE].rearrange("p (t e) -> p t e", t=NT), cum[:, 0:NT, :], ALU.add))
                link(dve.tensor_tensor(pos, pos, across(cst[:, 0, EPG:]), ALU.add))
                for k in range(2):
                    link(dve.tensor_tensor(prod, A[k], pos, ALU.mult))
                    link(dve.reduce_sum(dest_f[:, k, :], prod, AX_X))
                dve.tensor_copy(dest, dest_f).then_inc(ent_ready, 1)
                link(dve.tensor_scalar(nb_i, cum[0:1, NT, :], float(P - 1), None, ALU.add))
                link(dve.tensor_scalar(nb_i, nb_i, 7, None, ALU.arith_shift_right))
                link(dve.tensor_copy(nb, nb_i))
                link(dve.tensor_tensor_scan(pend, onesr, nb, 0.0, ALU.mult, ALU.add))
                link(dve.tensor_tensor(cmp_, pend.unsqueeze(1).to_broadcast([1, NTAB, NE]),
                                       bi.unsqueeze(2).to_broadcast([1, NTAB, NE]), ALU.is_le))
                link(dve.reduce_sum(be, cmp_, AX_X))
                link(dve.tensor_tensor(cmpe, cmp_, pend.unsqueeze(1).to_broadcast([1, NTAB, NE]), ALU.mult))
                link(dve.tensor_reduce(bs, cmpe, AX_X, ALU.max))
                link(dve.tensor_scalar(be, be, float(NE - 1), None, ALU.min))
                link(dve.tensor_tensor(bb, bi, bs, ALU.subtract))
                link(dve.tensor_tensor(new, bi, bs, ALU.is_equal))
                link(dve.tensor_scalar(bb, bb, float(P), None, ALU.mult))
                link(dve.scalar_tensor_tensor(out=bb, in0=be, scalar=float(CAP), in1=bb, op0=ALU.mult, op1=ALU.add))
                link(dve.tensor_scalar(bb, bb, float(NE * CAP - P), None, ALU.min))
                dve.tensor_copy(tab[:, 0, :], be)
                dve.tensor_copy(tab[:, 1, :], bb)
                dve.tensor_copy(tab[:, 3, :], new)
                link(dve.tensor_copy(tab[:, 2, :], pend[:, NE - 1:NE].to_broadcast([1, NTAB])))
                dve.sem_inc(tab_ready, 1)

            @block.gpsimd
            def _(pool):
                pool.memset(half, -0.5)
                pool.iota(pad[:, :, 0].bitcast(I32), pattern=[[0, CAP * NE // P // P], [1, P]], base=T, channel_multiplier=0)
                pool.memset(pad[:, :, 1], 0.0)
                pool.iota(ids, pattern=[[P, NT]], base=0, channel_multiplier=1).then_inc(ids_done, 1)
                pool.wait_ge(ids_done, 1)
                pool.dma_start(a["slots"].rearrange("(p c) two -> p c two", p=P), pad).then_inc(slots_set, 16)
                pool.wait_ge(sq_done, NT)
                pool.tensor_scalar(rs, ss, 1.0 / D, EPS, ALU.mult, ALU.add).then_inc(pstep, 1)
                pool.wait_ge(pstep, 1)
                pool.tensor_tensor(rs, rs, half, ALU.pow).then_inc(rs_done, 1)
                pool.wait_ge(ent_ready, 1)
                pool.wait_ge(slots_set, 16)
                for k in range(2):
                    for t in range(NT):
                        pool.indirect_dma_start(a["slots"], bass.IndirectOffsetOnAxis(ap=dest[:, k, t:t + 1], axis=0),
                                                ent[:, k, t, :], None).then_inc(list_out, 16)
                pool.wait_ge(list_out, 2 * NT * 16)


def experts(nc, a):
    with ExitStack() as ctx:
        def sb(name, shape, dt=F32):
            return ctx.enter_context(nc.sbuf_tensor(name, shape, dt))[...]

        def sem(name):
            return ctx.enter_context(nc.semaphore(name))

        wg, wu, wd = sb("e_wg", [P, KT, DE]), sb("e_wu", [P, KT, DE]), sb("e_wd", [P, DE // P, D])
        tab = sb("e_tab", [1, 4, NTAB], I32)
        ident, g_ffn, half = sb("e_ident", [P, P]), sb("e_g", [P, KT]), sb("e_half", [P, 1])
        ring = sb("e_ring", [P, 4, 2])
        nxt, prv = sb("e_nxt", [P, 2]), sb("e_prv", [P, 2])
        xg, junk = sb("e_xg", [P, D]), sb("e_junk", [P, D])
        ss, ms, rs, hrs, hrs2 = (sb(f"e_{n}", [P, 1]) for n in ("ss", "ms", "rs", "hrs", "hrs2"))
        xT = sb("e_xT", [P, KT, P])
        th, hid, hidT = sb("e_th", [P, DE]), sb("e_hid", [P, DE]), sb("e_hidT", [P, DE // P, P])
        yo = sb("e_yo", [P, D])
        ps_g, ps_u, ps_h = (ctx.enter_context(nc.psum_tensor(f"e_ps{n}", [P, 512], F32)) for n in "guh")
        ps_x = [ctx.enter_context(nc.psum_tensor(f"e_psx{i}", [P, 512], F32)) for i in range(2)]
        ps_y = [ctx.enter_context(nc.psum_tensor(f"e_psy{i}", [P, 512], F32)) for i in range(2)]

        tab_in, const_in, set_done = sem("e_tab_in"), sem("e_const_in"), sem("e_set_done")
        wg_in, wu_in, wd_in = ([sem(f"e_{n}_in{h}") for h in range(2)] for n in ("wg", "wu", "wd"))
        slots_in, x_in, y_out = sem("e_slots_in"), sem("e_x_in"), sem("e_y_out")
        g_ps, u_ps, x_ps, y_ps, h_ps = sem("e_g_ps"), sem("e_u_ps"), sem("e_x_ps"), sem("e_y_ps"), sem("e_h_ps")
        xT_done, tanh_done, glu_done, hid_done, hidT_done, yo_done = (
            sem("e_xT_done"), sem("e_tanh_done"), sem("e_glu_done"), sem("e_hid_done"), sem("e_hidT_done"), sem("e_yo_done"))
        ss_done, rs_done, shifted, pstep, settled = (
            sem("e_ss_done"), sem("e_rs_done"), sem("e_shifted"), sem("e_pstep"), sem("e_settled"))

        with nc.Block() as block:

            def blocks(eng):
                eng.wait_ge(tab_in, 16)
                return eng.value_load(tab[0:1, 2, 0:1], min_val=2 * T // P, max_val=MAXB)

            @block.sync
            def _(sp):
                reads = {"w_gate_e": g_ps, "w_up_e": u_ps, "w_down_e": y_ps}
                sp.dma_start(tab, a["table"]).then_inc(tab_in, 16)
                sp.dma_start(ident, a["ident"]).then_inc(const_in, 16)
                sp.dma_start(g_ffn, a["norm_ffn_g"]).then_inc(const_in, 16)
                n = blocks(sp)

                def load(i, dst, name, w_in):
                    e = sp.value_load(tab[0:1, 0, bass.ds(i, 1)], min_val=0, max_val=NE - 1)
                    new = sp.value_load(tab[0:1, 3, bass.ds(i, 1)], min_val=0, max_val=1)
                    k = dst.shape[1] // 2
                    for h in range(2):
                        if not isinstance(i, int):
                            sp.wait_ge(reads[name], i * 2 + (h + (3 if name == "w_down_e" else -1)))
                            sp.sem_inc(settled, 1)
                        elif i:
                            sp.wait_ge(reads[name], i * 2 + h - 1)
                        src = a[name][bass.ds(e, 1), h * k * P:(h + 1) * k * P, :].rearrange("o (k p) c -> p (o k) c", p=P)
                        sp.dma_start(dst[:, h * k:(h + 1) * k, :], src, cond=None if isinstance(i, int) and not i else new,
                                     bounds_check=None).then_inc(w_in[h], 16)

                load(0, wg, "w_gate_e", wg_in)
                load(0, wu, "w_up_e", wu_in)
                load(0, wd, "w_down_e", wd_in)
                load(1, wg, "w_gate_e", wg_in)
                load(1, wu, "w_up_e", wu_in)
                with sp.Fori(1, n - 1) as i:
                    load(i + 1, wg, "w_gate_e", wg_in)
                    load(i + 1, wu, "w_up_e", wu_in)
                    load(i, wd, "w_down_e", wd_in)
                load(n - 1, wd, "w_down_e", wd_in)

            @block.tensor
            def _(pe):
                n = blocks(pe)
                pe.wait_ge(const_in, 32)

                def turn_x(i):
                    pe.wait_ge(x_in, (i + 1) * 16)
                    for b in range(2):
                        for k in range(4):
                            c = (4 * b + k) * P
                            mm = pe.transpose(ps_x[b][:, k * P:(k + 1) * P], xg[:, c:c + P], ident)
                        mm.then_inc(x_ps, 1)

                def gate_up(i):
                    pe.wait_ge(xT_done, i * 2 + 2)
                    for w, ps, w_in, done in ((wg, ps_g, wg_in, g_ps), (wu, ps_u, wu_in, u_ps)):
                        for k in range(KT):
                            if k % 4 == 0:
                                pe.wait_ge(w_in[k // 4], (i + 1) * 16)
                            mm = pe.matmul(ps[:], xT[:, k, :], w[:, k, :], start=(k == 0), stop=(k == KT - 1))
                            if k % 4 == 3:
                                mm.then_inc(done, 1)

                def down(i):
                    pe.wait_ge(hidT_done, i + 1)
                    for k in range(DE // P):
                        if k % 2 == 0:
                            pe.wait_ge(wd_in[k // 2], (i + 1) * 16)
                        for h in range(2):
                            mm = pe.matmul(ps_y[h][:], hidT[:, k, :], wd[:, k, h * 512:(h + 1) * 512], start=(k == 0),
                                           stop=(k == DE // P - 1))
                        if k % 2:
                            mm.then_inc(y_ps, 1)

                def turn_hidden(i):
                    pe.wait_ge(hid_done, i + 1)
                    for k in range(DE // P):
                        mm = pe.transpose(ps_h[:, k * P:(k + 1) * P], hid[:, k * P:(k + 1) * P], ident)
                    mm.then_inc(h_ps, 1)

                pe.sem_inc(y_ps, 4)
                turn_x(0)
                gate_up(0)
                turn_x(1)
                turn_hidden(0)
                with pe.Fori(1, n) as i:
                    gate_up(i)
                    turn_x(i + 1)
                    pe.wait_ge(yo_done, i * 2)
                    down(i - 1)
                    turn_hidden(i)
                pe.wait_ge(yo_done, n * 2)
                down(n - 1)

            @block.scalar
            def _(act):
                n = blocks(act)

                def squares(i):
                    act.wait_ge(x_in, (i + 1) * 16)
                    act.activation(junk, xg, ACT.Square, accum_out=ss).then_inc(ss_done, 1)

                def tanh(i):
                    act.wait_ge(g_ps, i * 2 + 2)
                    act.wait_ge(rs_done, i + 1)
                    act.activation(th, ps_g[:], ACT.Tanh, scale=hrs).then_inc(tanh_done, 1)

                def hidden(i):
                    act.wait_ge(h_ps, i + 1)
                    act.activation(hidT, ps_h[:].rearrange("p (k q) -> p k q", k=DE // P), ACT.Copy).then_inc(hidT_done, 1)

                squares(0)
                tanh(0)
                act.wait_ge(ss_done, 1)
                squares(1)
                hidden(0)
                with act.Fori(1, n) as i:
                    tanh(i)
                    act.wait_ge(ss_done, i + 1)
                    squares(i + 1)
                    act.wait_ge(y_ps, i * 2 + 4)
                    hidden(i)

            @block.vector
            def _(dve):
                n = blocks(dve)
                dve.wait_ge(const_in, 32)
                dve.sem_inc(yo_done, 2)

                def copy_x(i):
                    for b in range(2):
                        dve.wait_ge(x_ps, i * 2 + (b + 1))
                        dve.tensor_tensor(xT[:, 4 * b:4 * b + 4, :], ps_x[b][:].rearrange("p (k q) -> p k q", k=4),
                                          g_ffn[:, 4 * b:4 * b + 4].unsqueeze(2).to_broadcast([P, 4, P]),
                                          ALU.mult).then_inc(xT_done, 1)

                def glu(i):
                    dve.wait_ge(tanh_done, i + 1)
                    dve.scalar_tensor_tensor(out=th, in0=th, scalar=1.0, in1=ps_g[:], op0=ALU.add, op1=ALU.mult).then_inc(glu_done, 1)
                    dve.wait_ge(glu_done, i + 1)
                    dve.wait_ge(u_ps, i * 2 + 2)
                    dve.scalar_tensor_tensor(out=hid, in0=th, scalar=hrs2, in1=ps_u[:], op0=ALU.mult, op1=ALU.mult).then_inc(hid_done, 1)

                def weigh(i):
                    dve.wait_ge(y_ps, i * 2 + 6)
                    dve.wait_ge(shifted, i + 1)
                    for h in range(2):
                        dve.tensor_scalar(yo[:, h * 512:(h + 1) * 512], ps_y[h][:], prv[:, 1:2], None, ALU.mult).then_inc(yo_done, 1)

                copy_x(0)
                glu(0)
                copy_x(1)
                with dve.Fori(1, n) as i:
                    glu(i)
                    copy_x(i + 1)
                    weigh(i - 1)
                weigh(n - 1)

            @block.gpsimd
            def _(pool):
                pool.memset(half, -0.5).then_inc(set_done, 1)
                n = blocks(pool)
                pool.wait_ge(set_done, 1)

                def load_slots(i):
                    first = pool.value_load(tab[0:1, 1, bass.ds(i, 1)], min_val=0, max_val=NE * CAP - P)
                    pool.dma_start(ring[:, i % 4, :] if isinstance(i, int) else ring[:, bass.ds(i % 4, 1), :],
                                   a["slots"][bass.ds(first, P), :]).then_inc(slots_in, 16)

                def entry(i):
                    return ring[:, i % 4, :] if isinstance(i, int) else ring[:, bass.ds(i % 4, 1), :].rearrange("p o c -> p (o c)")

                def gather(i, copied):
                    pool.wait_ge(slots_in, i * 16 + 16)
                    pool.sem_inc(settled, 1)
                    pool.tensor_copy(nxt, entry(i)).then_inc(pstep, 1)
                    pool.wait_ge(pstep, copied)
                    pool.sem_inc(settled, 1)
                    pool.indirect_dma_start(xg, None, a["x2s"], bass.IndirectOffsetOnAxis(ap=nxt[:, 0:1].bitcast(I32), axis=0)).then_inc(x_in, 16)

                def root(i, link):
                    pool.wait_ge(ss_done, i + 1)
                    pool.sem_inc(settled, 1)
                    pool.tensor_scalar(ms, ss, 1.0 / D, EPS, ALU.mult, ALU.add).then_inc(pstep, 1)
                    pool.wait_ge(pstep, link(1))
                    pool.tensor_tensor(rs, ms, half, ALU.pow).then_inc(pstep, 1)
                    pool.wait_ge(pstep, link(2))
                    pool.sem_inc(settled, 1)
                    pool.tensor_scalar(hrs, rs, 0.5, 1.0, ALU.mult, ALU.mult).then_inc(pstep, 1)
                    pool.wait_ge(pstep, link(3))
                    pool.tensor_tensor(hrs2, hrs, rs, ALU.mult).then_inc(rs_done, 1)

                def scatter():
                    pool.indirect_dma_start(a["y"], bass.IndirectOffsetOnAxis(ap=prv[:, 0:1].bitcast(I32), axis=0), yo, None,
                                            compute_op=ALU.add).then_inc(y_out, 16)

                load_slots(0)
                pool.iota(prv[:, 0:1].bitcast(I32), pattern=[[0, 1]], base=T, channel_multiplier=1)
                pool.memset(yo, 0.0).then_inc(pstep, 1)
                pool.wait_ge(pstep, 1)
                scatter()
                gather(0, 2)
                load_slots(1)
                root(0, lambda k: 2 + k)
                pool.wait_ge(x_ps, 2)
                pool.wait_ge(x_in, 16)
                gather(1, 6)
                load_slots(2)
                pool.wait_ge(hid_done, 1)
                root(1, lambda k: 6 + k)
                with pool.Fori(1, n) as i:
                    pool.wait_ge(x_ps, i * 2 + 2)
                    pool.wait_ge(x_in, i * 16 + 16)
                    gather(i + 1, i * 4 + 6)
                    load_slots(i + 2)
                    pool.wait_ge(y_out, i * 16)
                    pool.sem_inc(settled, 1)
                    pool.tensor_copy(prv, entry(i + 3)).then_inc(shifted, 1)
                    pool.wait_ge(hid_done, i + 1)
                    root(i + 1, lambda k: i * 4 + (6 + k))
                    pool.wait_ge(shifted, i)
                    pool.wait_ge(yo_done, i * 2 + 2)
                    pool.sem_inc(settled, 1)
                    scatter()
                pool.wait_ge(y_out, n * 16)
                pool.sem_inc(settled, 1)
                pool.tensor_copy(prv, entry(n + 3)).then_inc(shifted, 1)
                pool.wait_ge(shifted, n)
                pool.wait_ge(yo_done, n * 2 + 2)
                pool.sem_inc(settled, 1)
                scatter()
                pool.wait_ge(y_out, n * 16 + 16)


_WEIGHTS = ["norm_mix_g", "w_in", "norm_v_g", "w_spatial", "b_spatial", "q_norm_g", "k_norm_g", "sink", "w_proj_a",
            "w_proj_b", "w_out", "norm_ffn_g", "w_router_group", "b_router_group", "w_router_expert",
            "b_router_expert", "w_gate_e", "w_up_e", "w_down_e"]


def tables():
    half = HD // 2
    inv = (np.float32(10000.0) ** (-np.arange(half, dtype=np.float32) / np.float32(half))).astype(np.float32)
    rope = np.zeros((NG + 1, P, 5, 2, half), np.float32)
    mask = np.zeros((NG + 1, P, 3, 3 * P), np.float32)
    q, k = np.arange(P)[:, None], np.arange(3 * P)[None, :] - P
    band = np.abs(k - q) <= P
    for g in range(NG + 1):
        start = max(g - 1, 0) * G
        length = S_PROMPT if g == 0 else S_SAMPLE
        for t in range(5):
            ang = (start + t * P + np.arange(P)).astype(np.float32)[:, None] * inv[None, :]
            rope[g, :, t, 0], rope[g, :, t, 1] = np.cos(ang), np.sin(ang)
        for m, block in enumerate((0, 1, GT - 1)):
            pos = start + block * P + k
            mask[g, :, m] = np.where(band & (pos >= 0) & (pos < length), 0.0, NEG)
    counts = np.zeros((2, EPG + NE), np.float32)
    counts[0, :EPG] = np.arange(EPG)
    counts[1, :EPG] = np.arange(EPG) - 100
    counts[0, EPG:] = np.arange(NE) * CAP
    return {"counts": counts.reshape(1, -1), "blocks": np.arange(NTAB, dtype=np.float32)[None, :],
            "upper": np.triu(np.ones((P, P), np.float32), 1), "ident": np.eye(P, dtype=np.float32), "rope": rope.reshape((NG + 1) * P, -1),
            "mask": mask.reshape((NG + 1) * P, -1)}


def kernel(x_prompt, x_sample, **weights):
    import concourse.bacc as bacc
    from concourse.bass_utils import run_bass_kernel_spmd

    xp, xs = np.asarray(x_prompt)[0], np.asarray(x_sample)[0]
    w = {name: np.asarray(weights[name])[0] for name in _WEIGHTS}
    arrays = {"x_all": np.concatenate([xp, xs, xp, xs[:P]])}
    arrays.update(tables())
    for name in ("norm_mix_g", "norm_v_g", "norm_ffn_g"):
        w[name] = np.ascontiguousarray(w[name].reshape(KT, P).T)
    for name in ("q_norm_g", "k_norm_g", "sink", "b_router_group", "b_router_expert"):
        w[name] = w[name][None, :]
    w["b_spatial"] = w["b_spatial"].reshape(1, -1)
    arrays.update(w)
    nc = bacc.Bacc("TRN2", target_bir_lowering=False, num_devices=1, dynamic_dma_scratch_size=4096)
    a = {}
    for name in arrays:
        arrays[name] = np.ascontiguousarray(arrays[name])
        a[name] = nc.dram_tensor(name, arrays[name].shape, mybir.dt.from_np(arrays[name].dtype), kind="ExternalInput").ap()
    a["y"] = nc.dram_tensor("y", (T + P, D), F32, kind="ExternalOutput").ap()
    a["x2s"] = nc.dram_tensor("x2s", (T + P, D), F32, kind="Internal").ap()
    a["slots"] = nc.dram_tensor("slots", (NE * CAP, 2), F32, kind="Internal").ap()
    a["table"] = nc.dram_tensor("table", (1, 4, NTAB), I32, kind="Internal").ap()
    build(nc, a)
    y = run_bass_kernel_spmd(nc, [arrays], core_ids=[0]).results[0]["y"]
    return y[None, :S_PROMPT], y[None, S_PROMPT:T]


def build(nc, a):
    mixers(nc, a)
    route(nc, a)
    experts(nc, a)
```

```python
from contextlib import ExitStack

import numpy as np

import concourse.bass as bass
from concourse import mybir

F32 = mybir.dt.float32
F32R = mybir.dt.float32r
I32 = mybir.dt.int32
ALU = mybir.AluOpType
ACT = mybir.ActivationFunctionType
AX_X = mybir.AxisListType.X

P = 128
D = 1024
KT = D // P
HD = 128
NH, NKV = 8, 2
REP = NH // NKV
S_PROMPT, S_SAMPLE = 512, 1024
T = S_PROMPT + S_SAMPLE
G = 512
NG = T // G
GT = G // P
NT = T // P
N_GROUPS, EPG = 4, 8
NE = N_GROUPS * EPG
DE = 512
MAXB = 2 * T // P + NE
NTAB = MAXB + 8
TW = 3
EPS = 1e-6
NEG = -1e30
BIG = 3e38

U0, V0, Q0, K0, VA0, GA0, GB0 = 0, 1024, 2048, 3072, 3328, 3584, 4608
PANELS = [("w_in", K0, 256), ("w_in", Q0, 512), ("w_in", Q0 + 512, 512), ("w_in", VA0, 256),
          ("w_in", GB0, 512), ("w_in", GB0 + 512, 512), ("w_proj_b", 0, 512), ("w_proj_b", 512, 512),
          ("w_in", V0, 512), ("w_in", V0 + 512, 512), ("w_in", U0, 512), ("w_in", U0 + 512, 512),
          ("w_in", GA0, 512), ("w_in", GA0 + 512, 512), ("w_proj_a", 0, 512), ("w_proj_a", 512, 512),
          ("w_out", 0, 512), ("w_out", 512, 512)]
PK, PQ, PVA, PGB, PPB, PV, PU, PGA, PPA, POUT = 0, 1, 3, 4, 6, 8, 10, 12, 14, 16
NP = len(PANELS)
NQ = 4
QPG = NP * NQ
NRAW = 3
NU = NH * GT
KT_AT = {(PQ, 2): 0, (PQ, 3): 1, (PQ + 1, 0): 2, (PQ + 1, 1): 3, (PQ + 1, 2): 4}
QT_AT = {(PQ + 1, 3): 0, (PVA, 0): 1, (PVA, 2): 2}
SPLIT_AT = [((0, 1), (2,), (3,), ())] * NP
SPLIT_AT[POUT] = ((0, 1, 2, 3), (), (), ())
PREP_AT = {1: (0, 1, 2), 2: (3, 4, 5), 3: (6, 7)}
SCALE = float(HD) ** -0.5


def slots_of(c):
    per, more = divmod(NU + 3, KT)
    start = per * c + min(c, more)
    return range(start, start + per + (c < more))


def mixers(nc, a):
    with ExitStack() as ctx:
        base = nc.sbuf_base + (-nc.sbuf_base) % 64
        arena = {"at": base}

        def place(name, shape, dt, at=None):
            size = int(np.prod(shape[1:])) * 4
            if at is None:
                at = arena["at"]
                arena["at"] += size + (-size) % 32
            return nc.alloc_sbuf_tensor_at(name, shape, dt, offset=at)[...], at

        hT_hi, _ = place("hT_hi", [P, KT, G], F32R)
        hT_lo, _ = place("hT_lo", [P, KT, G], F32R)
        hx_hi, _ = place("hx_hi", [P, KT, P], F32R)
        hx_lo, _ = place("hx_lo", [P, KT, P], F32R)
        w_hi = [place(f"w_hi{i}", [P, KT, 512], F32R)[0] for i in range(2)]
        w_lo = [place(f"w_lo{i}", [P, KT, 512], F32R)[0] for i in range(2)]
        raw = [place(f"raw{i}", [P, 1024], F32)[0] for i in range(NRAW)]
        kT, _ = place("kT", [P, NKV, 6 * P], F32)
        va, _ = place("va", [P, 6, NKV * HD], F32)
        A, B, C, Dd = (place(f"region{i}", [P, 4096], F32)[1] for i in range(4))
        T1, T2 = (place(f"temp{i}", [P, 1024], F32)[1] for i in range(2))
        qT, _ = place("qT", [P, NH, G], F32, A)
        oT_hi, _ = place("oT_hi", [P, NH, G], F32R, A)
        ws, _ = place("ws", [P, NH, P], F32, A)
        vn, _ = place("vn", [P, GT, D], F32, A)
        sga, _ = place("sga", [P, KT, G], F32, A)
        m_lo, _ = place("m_lo", [P, KT, G], F32R, A)
        qn, _ = place("qn", [P, 2, GT, 512], F32, B)
        oT_lo, _ = place("oT_lo", [P, NH, G], F32R, B)
        uT, _ = place("uT", [P, KT, G], F32, B)
        aT_hi, _ = place("aT_hi", [P, KT, G], F32R, B)
        x2, _ = place("x2", [P, GT, D], F32, B)
        sgb, _ = place("sgb", [P, KT, G], F32, C)
        m_hi, _ = place("m_hi", [P, KT, G], F32R, C)
        xn, _ = place("xn", [P, GT, D], F32, Dd)
        kn, _ = place("kn", [P, 5, 256], F32, Dd)
        sq, _ = place("sq", [P, 512], F32, Dd + 5120)
        rot, _ = place("rot", [P, 512], F32, Dd + 7168)
        pt = [place(f"pt{i}", [P, 3 * P], F32, Dd + 1536 * i)[0] for i in range(2)]
        sm = [place("sm0", [P, 3 * P], F32, Dd + 3072)[0], place("sm1", [P, 3 * P], F32, Dd + 9216)[0]]
        pr = [place(f"pr{i}", [P, 3 * P], F32, Dd + 10752 + 1536 * i)[0] for i in range(3)]
        aT_lo, _ = place("aT_lo", [P, KT, G], F32R, Dd)
        xh, _ = place("xh", [P, D], F32, T1)
        bsp, _ = place("bsp", [P, NH, P], F32, T1)
        junk, _ = place("junk", [P, D], F32, T2)
        rot_v, _ = place("rot_v", [P, 512], F32, T2)
        tmp = [place(f"tmp{i}", [P, G], F32, T2 + 2048 * i)[0] for i in range(2)]
        mask, _ = place("mask", [P, 3, 3 * P], F32)
        rope, _ = place("rope", [P, 5, 2, HD // 2], F32)
        ident, _ = place("ident", [P, P], F32)
        wsT, _ = place("wsT", [P, NH, P], F32)
        gq, _ = place("gq", [P, HD], F32)
        gk, _ = place("gk", [P, HD], F32)
        g_mix, _ = place("g_mix", [P, KT], F32)
        g_v, _ = place("g_v", [P, KT], F32)
        sink, _ = place("sink", [P, NH], F32)
        nsink, _ = place("nsink", [P, NH], F32)
        half, _ = place("half", [P, 8], F32)
        ssx, _ = place("ssx", [P, 8], F32)
        rsx, _ = place("rsx", [P, 8], F32)
        ssq, _ = place("ssq", [P, 8], F32)
        rsq, _ = place("rsq", [P, 8], F32)
        ssv, _ = place("ssv", [P, GT, 2], F32)
        rsv, _ = place("rsv", [P, GT], F32)
        stat, _ = place("stat", [P, 4, 8], F32)
        assert arena["at"] <= nc.sbuf_usable_end, (arena["at"], nc.sbuf_usable_end)

        main = [ctx.enter_context(nc.psum_tensor(f"main{i}", [P, 512], F32)) for i in range(4)]
        aux = [ctx.enter_context(nc.psum_tensor(f"aux{i}", [P, 512], F32)) for i in range(4)]

        def sem(name):
            return ctx.enter_context(nc.semaphore(name))

        raw_in = [sem(f"raw_in{i}") for i in range(NRAW)]
        w_hi_done, w_split, out_ready = sem("w_hi_done"), sem("w_split"), sem("out_ready")
        const_in, const_set, ws_in, ws_ps, ws_done = sem("const_in"), sem("const_set"), sem("ws_in"), sem("ws_ps"), sem("ws_done")
        x_in, xh_in, table_in, bsp_in, x2_in = (
            sem("x_in"), sem("xh_in"), sem("table_in"), sem("bsp_in"), [sem(f"x2_in{i}") for i in range(2)])
        ssx_ready, rsx_ready, xn_ready, hT_ps, hT_hi_done, hT_done = (
            sem("ssx_ready"), sem("rsx_ready"), sem("xn_ready"), sem("hT_ps"), sem("hT_hi_done"), sem("hT_done"))
        hx_ps, hx_mul, hx_hi_done, hx_done = sem("hx_ps"), sem("hx_mul"), sem("hx_hi_done"), sem("hx_done")
        halo_ready, sq_ready, ssq_ready, rsq_ready, head_normed, head_roped, q1_roped, rope_step = (
            sem("halo_ready"), sem("sq_ready"), sem("ssq_ready"), sem("rsq_ready"), sem("head_normed"), sem("head_roped"),
            sem("q1_roped"), sem("rope_step"))
        kT_ps, kT_done, va_done, qT_ps, qT_done, halo_kept = (
            sem("kT_ps"), sem("kT_done"), sem("va_done"), sem("qT_ps"), sem("qT_done"), sem("halo_kept"))
        s_ps, s_masked, negm_ready, exp_done, rden_ready, p_ready = (
            sem("s_ps"), sem("s_masked"), sem("negm_ready"), sem("exp_done"), sem("rden_ready"), sem("p_ready"))
        pt_ps, pt_ready, o_ps, o_hi_done, o_done = sem("pt_ps"), sem("pt_ready"), sem("o_ps"), sem("o_hi_done"), sem("o_done")
        tanh_b, sgb_ready, mb_done, tanh_a, sga_ready = sem("tanh_b"), sem("sgb_ready"), sem("mb_done"), sem("tanh_a"), sem("sga_ready")
        gelu_v, ssv_ready, rsv_ready, vn_ready, uT_ready = sem("gelu_v"), sem("ssv_ready"), sem("rsv_ready"), sem("vn_ready"), sem("uT_ready")
        sp_ps, mixed_ready, a_ready, a_hi_done, a_done = sem("sp_ps"), sem("mixed_ready"), sem("a_ready"), sem("a_hi_done"), sem("a_done")
        ya_gated, m_ready, m_hi_done, m_done = sem("ya_gated"), sem("m_ready"), sem("m_hi_done"), sem("m_done")
        x2_done, y_out = sem("x2_done"), sem("y_out")
        pool_step, dve_step, settled = sem("pool_step"), sem("dve_step"), sem("settled")

        def quarter(i):
            p, q = divmod(i % QPG, NQ)
            name, c, n = PANELS[p]
            src = a[name][256 * q:256 * q + 256, c:c + n].rearrange("(k p) c -> p k c", p=P)
            buf = raw[i % NRAW][:, 0:2 * n].rearrange("p (k c) -> p k c", k=2)
            return src, buf, w_hi[p % 2][:, 2 * q:2 * q + 2, 0:n], w_lo[p % 2][:, 2 * q:2 * q + 2, 0:n]

        with nc.Block() as block:

            @block.sync
            def _(sp):
                sp.dma_start(ident, a["ident"]).then_inc(const_in, 16)
                sp.dma_start(g_mix, a["norm_mix_g"]).then_inc(const_in, 16)
                for i in range(NRAW):
                    src, buf, _, _ = quarter(i)
                    sp.dma_start(buf, src).then_inc(raw_in[i], 16)
                sp.dma_start(g_v, a["norm_v_g"]).then_inc(const_in, 16)
                for dst, name, n in ((gq, "q_norm_g", HD), (gk, "k_norm_g", HD), (sink, "sink", NH)):
                    sp.dma_start(dst, a[name].to_broadcast([P, n])).then_inc(const_in, 16)
                with sp.Fori(0, NG) as g:
                    for i in range(QPG):
                        sp.wait_ge(w_split, g * QPG + (i + 1))
                        src, buf, _, _ = quarter(i + NRAW)
                        sp.dma_start(buf, src).then_inc(raw_in[(i + NRAW) % NRAW], 16)
                sp.wait_ge(w_split, NG * QPG + 1)
                src, buf, _, _ = quarter(NRAW)
                sp.dma_start(buf, src).then_inc(raw_in[0], 16)

            @block.tensor
            def _(pe):
                readers = {PK: (head_normed, 13, 0), PVA: (va_done, 5, 0), PQ: (head_normed, 13, 5),
                           PQ + 1: (head_normed, 13, 9), PGB: (tanh_b, KT, 0), PGB + 1: (tanh_b, KT, 4),
                           PPB: (mb_done, KT, 0), PPB + 1: (mb_done, KT, 4), PV: (gelu_v, 8, 0), PV + 1: (gelu_v, 8, 4),
                           PU: (uT_ready, KT, 0), PU + 1: (uT_ready, KT, 4), PGA: (tanh_a, KT, 0),
                           PGA + 1: (tanh_a, KT, 4), PPA: (ya_gated, KT, 0), PPA + 1: (ya_gated, KT, 4),
                           POUT: (x2_done, 8, 8), POUT + 1: (x2_done, 8, 12)}
                last = [None] * 4

                def take(b, g, reader, per, n):
                    if last[b] is not None:
                        sem_, per_, n_ = last[b]
                        pe.wait_ge(sem_, g * per_ + n_)
                    last[b] = (reader, per, n)
                    return aux[b]

                def transpose_h(g, k, ahead):
                    bank = take(k % 4, g, hT_done, KT, ahead * KT + k + 1)
                    for t in range(GT):
                        mm = pe.transpose(bank[:, t * P:(t + 1) * P], xn[:, t, k * P:(k + 1) * P], ident)
                    mm.then_inc(hT_ps, 1)

                def transpose_halo(g, ahead):
                    for b in range(2):
                        bank = take(b, g, hx_done, 2, 2 * ahead + b + 1)
                        for k in range(4):
                            c = (4 * b + k) * P
                            mm = pe.transpose(bank[:, k * P:(k + 1) * P], xh[:, c:c + P], ident)
                        mm.then_inc(hx_ps, 1)

                pe.wait_ge(ws_in, 16)
                pe.wait_ge(const_in, 96)
                for b in range(2):
                    for k in range(4):
                        mm = pe.transpose(aux[b][:, k * P:(k + 1) * P],
                                          ws[:, 4 * b + k, :], ident)
                    mm.then_inc(ws_ps, 1)
                    last[b] = (ws_done, 0, b + 1)
                pe.wait_ge(xn_ready, 5)
                for k in range(KT):
                    transpose_h(0, k, 0)
                transpose_halo(0, 0)

                def token_major(bank, stat_hi, stat_lo, p, ready=None):
                    n = PANELS[p][2]
                    hi, lo = w_hi[p % 2], w_lo[p % 2]
                    for k in range(KT):
                        if ready is not None:
                            ready(k)
                        pe.matmul(bank[:, 0:n], stat_hi(k), hi[:, k, 0:n], start=(k == 0), stop=False)
                        pe.matmul(bank[:, 0:n], stat_hi(k), lo[:, k, 0:n], start=False, stop=False)
                        mm = pe.matmul(bank[:, 0:n], stat_lo(k), hi[:, k, 0:n], start=False, stop=(k == KT - 1))
                    return mm

                def feature_major(g, bank, mov_hi, mov_lo, p, j, ready=None, slots=()):
                    slots = list(slots)
                    hi, lo = w_hi[p % 2][:, :, j * P:(j + 1) * P], w_lo[p % 2][:, :, j * P:(j + 1) * P]
                    for k in range(KT):
                        if ready is not None:
                            ready(k)
                        pe.matmul(bank[:], hi[:, k, :], mov_hi[:, k, :], start=(k == 0), stop=False)
                        pe.matmul(bank[:], hi[:, k, :], mov_lo[:, k, :], start=False, stop=False)
                        mm = pe.matmul(bank[:], lo[:, k, :], mov_hi[:, k, :], start=False, stop=(k == KT - 1))
                        for s in slots[k * len(slots) // KT:(k + 1) * len(slots) // KT]:
                            attend(g, s)
                    return mm

                def kT_tile(g, t):
                    pe.wait_ge(head_roped, g * 9 + (t + 1))
                    bank = take(2 + t % 2, g, kT_done, 5, t + 1)
                    for h in range(NKV):
                        mm = pe.transpose(bank[:, h * P:(h + 1) * P], kn[:, t, h * P:(h + 1) * P], ident)
                    mm.then_inc(kT_ps, 1)

                def qT_tile(g, i):
                    if i < GT:
                        pe.wait_ge(head_roped, g * 9 + (5 + i + 1))
                    else:
                        pe.wait_ge(q1_roped, g * GT + (i - GT + 1))
                    bank = take(2 + i % 2, g, qT_done, 8, i + 1)
                    for h in range(4):
                        mm = pe.transpose(bank[:, h * P:(h + 1) * P], qn[:, i // GT, i % GT, h * P:(h + 1) * P], ident)
                    mm.then_inc(qT_ps, 1)

                def attend(g, s):
                    if s < NU:
                        h, n = divmod(s, GT)
                        if s == 0:
                            pe.wait_ge(kT_done, g * 5 + 5)
                            pe.wait_ge(va_done, g * 5 + 5)
                            pe.wait_ge(halo_kept, g + 1)
                        if s % 16 == 0:
                            pe.wait_ge(qT_done, g * 8 + (s // 4 + 4))
                        bank = take(s % 2, g, s_masked, NU, s + 1)
                        pe.matmul(bank[:, 0:3 * P], qT[:, h, n * P:(n + 1) * P],
                                  kT[:, h // REP, n * P:(n + 3) * P], start=True, stop=True).then_inc(s_ps, 1)
                    if 0 <= s - 2 < NU:
                        u = s - 2
                        pe.wait_ge(p_ready, g * NU + (u + 1))
                        bank = take(2, g, pt_ready, NU, u + 1)
                        for c in range(3):
                            mm = pe.transpose(bank[:, c * P:(c + 1) * P], pr[u % 3][:, c * P:(c + 1) * P], ident)
                        mm.then_inc(pt_ps, 1)
                    if 0 <= s - 3 < NU:
                        u = s - 3
                        h, n = divmod(u, GT)
                        pe.wait_ge(pt_ready, g * NU + (u + 1))
                        bank = take(3, g, o_done, NU, u + 1)
                        for c in range(3):
                            v = va[:, n + c, (h // REP) * HD:(h // REP + 1) * HD]
                            mm = pe.matmul(bank[:, 0:P], v, pt[u % 2][:, c * P:(c + 1) * P], start=(c == 0), stop=(c == 2))
                        mm.then_inc(o_ps, 1)

                def spatial(g, c):
                    bank = take(c % 4, g, mixed_ready, KT, c + 1)
                    for n in range(GT):
                        mm = pe.matmul(bank[:, n * P:(n + 1) * P], vn[:, n, c * P:(c + 1) * P], wsT[:, c, :],
                                       start=True, stop=True)
                    mm.then_inc(sp_ps, 1)

                with pe.Fori(0, NG) as g:
                    for p in range(NP):
                        if p == PK:
                            pe.wait_ge(hT_done, g * KT + KT)
                        def ready(k, p=p):
                            if p == PPB:
                                pe.wait_ge(o_done, g * NU + (k + 1) * GT)
                            else:
                                pe.wait_ge(a_done if p == PPA else m_done, g * KT + (k + 1))
                        if p == PU + 1:
                            pe.wait_ge(vn_ready, g * GT + GT)
                        if p == PGA:
                            for c in range(4, 8):
                                spatial(g, c)
                        pe.wait_ge(w_split, g * QPG + NQ * (p + 1))
                        for j in range(4):
                            if (p, j) in KT_AT:
                                kT_tile(g, KT_AT[p, j])
                            if (p, j) in QT_AT:
                                qT_tile(g, QT_AT[p, j])
                            if p == PGB:
                                qT_tile(g, 4 + j)
                            if p == PU + 1:
                                spatial(g, j)
                            if p == POUT + 1 and j:
                                if j == 1:
                                    pe.wait_ge(xn_ready, g * 5 + 10)
                                for k in PREP_AT[j]:
                                    transpose_h(g, k, 1)
                                if j == 3:
                                    transpose_halo(g, 1)
                            reader, per, n = readers[p - 1] if p else (x2_done, 8, 4)
                            pe.wait_ge(reader, g * per + (n + j + 1))
                            bank = main[j]
                            if p in (PK, PVA, PQ, PQ + 1, PV, PV + 1):
                                mm = token_major(bank, lambda k: hT_hi[:, k, j * P:(j + 1) * P],
                                                 lambda k: hT_lo[:, k, j * P:(j + 1) * P], p)
                            elif p >= POUT:
                                mm = token_major(bank, lambda k: m_hi[:, k, j * P:(j + 1) * P],
                                                 lambda k: m_lo[:, k, j * P:(j + 1) * P], p,
                                                 ready if p == POUT and j == 0 else None)
                            elif p in (PPB, PPB + 1):
                                mm = feature_major(g, bank, oT_hi, oT_lo, p, j, ready if p == PPB and j == 0 else None)
                            elif p in (PPA, PPA + 1):
                                mm = feature_major(g, bank, aT_hi, aT_lo, p, j, ready if p == PPA and j == 0 else None)
                            else:
                                mm = feature_major(g, bank, hT_hi, hT_lo, p, j,
                                                   slots=slots_of(4 * (p - PGB) + j) if p in (PGB, PGB + 1) else ())
                            mm.then_inc(out_ready, 1)
                        if p in (PK, PVA):
                            if p == PK:
                                pe.wait_ge(hx_done, g * 2 + 2)
                            bank = take(int(p == PVA), g, *((head_normed, 13, 5) if p == PK else (va_done, 5, 5)))
                            token_major(bank, lambda k: hx_hi[:, k, :], lambda k: hx_lo[:, k, :], p).then_inc(halo_ready, 1)
                        if p == PVA:
                            qT_tile(g, GT - 1)

            @block.scalar
            def _(act):
                def split_hi(g, i):
                    _, buf, hi, _ = quarter(i)
                    act.wait_ge(raw_in[i % NRAW], (g * (QPG // NRAW) + (i // NRAW + 1)) * 16)
                    p = i // NQ - 2
                    if p in (PK, PVA):
                        act.wait_ge(halo_ready, g * 2 + (1 if p == PK else 2))
                    elif p >= 0:
                        act.wait_ge(out_ready, g * 4 * NP + 4 * (p + 1))
                    act.activation(hi, buf, ACT.Copy).then_inc(w_hi_done, 1)

                def prep(n, k):
                    if k < 0:
                        act.wait_ge(x_in, n * 16 + 16)
                        for t in range(GT):
                            if t:
                                act.wait_ge(ssx_ready, n * 5 + t)
                            act.activation(junk, xn[:, t, :], ACT.Square, accum_out=ssx[:, t:t + 1]).then_inc(ssx_ready, 1)
                        act.wait_ge(xh_in, n * 16 + 16)
                        act.wait_ge(ssx_ready, n * 5 + 4)
                        act.activation(junk, xh, ACT.Square, accum_out=ssx[:, 4:5]).then_inc(ssx_ready, 1)
                    elif k < KT:
                        act.wait_ge(hT_ps, n * KT + (k + 1))
                        act.activation(hT_hi[:, k, :], aux[k % 4][:], ACT.Copy, scale=g_mix[:, k:k + 1]).then_inc(hT_hi_done, 1)
                    else:
                        b = k - KT
                        act.wait_ge(hx_ps, n * 2 + (b + 1))
                        for i in range(4):
                            ins = act.activation(hx_hi[:, 4 * b + i, :], aux[b][:, i * P:(i + 1) * P], ACT.Copy,
                                                 scale=g_mix[:, 4 * b + i:4 * b + i + 1])
                        ins.then_inc(hx_hi_done, 1)

                prep(0, -1)
                act.wait_ge(const_in, 96)
                for b in range(2):
                    act.wait_ge(ws_ps, b + 1)
                    act.activation(wsT[:, 4 * b:4 * b + 4, :], aux[b][:].rearrange("p (k q) -> p k q", k=4),
                                   ACT.Copy).then_inc(ws_done, 1)
                act.activation(nsink, sink, ACT.Copy, scale=-1.0)
                for i in range(NQ):
                    split_hi(0, i)
                for k in range(KT + 2):
                    prep(0, k)

                def attend(g, s):
                    if 0 <= s - 2 < NU:
                        u = s - 2
                        act.wait_ge(pt_ps, g * NU + (u + 1))
                        if u >= 2:
                            act.wait_ge(o_ps, g * NU + (u - 1))
                        ins = act.activation(pt[u % 2], aux[2][:, 0:3 * P], ACT.Copy)
                        ins.then_inc(pt_ready, 1)
                    if s < NU:
                        h = s // GT
                        act.wait_ge(negm_ready, g * NU + (s + 1))
                        if s >= 3:
                            act.wait_ge(pt_ps, g * NU + (s - 2))
                        act.activation(pr[s % 3], sm[s % 2], ACT.Exp, bias=stat[:, s % 4, 1:2], scale=SCALE,
                                       accum_out=stat[:, s % 4, 2:3])
                        act.activation(stat[:, s % 4, 3:4], stat[:, s % 4, 1:2], ACT.Exp,
                                       bias=sink[:, h:h + 1]).then_inc(exp_done, 1)
                    if 0 <= s - 3 < NU:
                        u = s - 3
                        h, n = divmod(u, GT)
                        act.wait_ge(o_ps, g * NU + (u + 1))
                        act.activation(oT_hi[:, h, n * P:(n + 1) * P], aux[3][:, 0:P], ACT.Copy).then_inc(o_hi_done, 1)

                def copy_kT(g, t):
                    act.wait_ge(kT_ps, g * 5 + (t + 1))
                    b = 2 + t % 2
                    act.activation(kT[:, :, (t + 1) * P:(t + 2) * P], aux[b][:, 0:2 * P].rearrange("p (h q) -> p h q", h=2),
                                   ACT.Copy).then_inc(kT_done, 1)

                def copy_qT(g, i):
                    act.wait_ge(qT_ps, g * 8 + (i + 1))
                    b, q, t = 2 + i % 2, i // GT, i % GT
                    act.activation(qT[:, 4 * q:4 * q + 4, t * P:(t + 1) * P], aux[b][:].rearrange("p (h q) -> p h q", h=4),
                                   ACT.Copy).then_inc(qT_done, 1)

                def round_a(g, c):
                    act.wait_ge(a_ready, g * KT + (c + 1))
                    act.activation(aT_hi[:, c, :], tmp[c % 2], ACT.Copy).then_inc(a_hi_done, 1)

                def round_m(g, c):
                    act.wait_ge(m_ready, g * KT + (c + 1))
                    act.activation(m_hi[:, c, :], tmp[c % 2], ACT.Copy).then_inc(m_hi_done, 1)

                with act.Fori(0, NG) as g:
                    for p in range(NP):
                        for j in range(4):
                            for q in SPLIT_AT[p][j]:
                                split_hi(g, NQ * (p + 1) + q)
                            if p == POUT and j == 1:
                                prep(g + 1, -1)
                            o = g * 4 * NP + (4 * p + j + 1)
                            if (p, j) in KT_AT:
                                copy_kT(g, KT_AT[p, j])
                            if (p, j) in QT_AT:
                                copy_qT(g, QT_AT[p, j])
                            if p == PGB:
                                copy_qT(g, 4 + j)
                            if p in (PGB, PGB + 1):
                                for s in slots_of(4 * (p - PGB) + j):
                                    attend(g, s)
                            if p == PGA:
                                round_a(g, 4 + j)
                            if p == PU + 1:
                                round_a(g, j)
                            if p == POUT + 1 and j:
                                for k in PREP_AT[j]:
                                    prep(g + 1, k)
                                if j == 3:
                                    prep(g + 1, KT)
                                    prep(g + 1, KT + 1)
                            if p in (PK, PQ, PQ + 1):
                                n = 256 if p == PK else 512
                                i = j if p == PK else 5 + 4 * (p - PQ) + j
                                act.wait_ge(out_ready, o)
                                if i:
                                    act.wait_ge(ssq_ready, g * 13 + i)
                                act.activation(sq[:, 0:n], main[j][:, 0:n], ACT.Square).then_inc(sq_ready, 1)
                            if p == PVA:
                                act.wait_ge(out_ready, o)
                                act.activation(va[:, j + 1, :], main[j][:, 0:256], ACT.Copy).then_inc(va_done, 1)
                            if p in (PGB, PGB + 1):
                                act.wait_ge(out_ready, o)
                                act.activation(sgb[:, 4 * (p - PGB) + j, :], main[j][:], ACT.Tanh, scale=0.5).then_inc(tanh_b, 1)
                            if p in (PV, PV + 1):
                                q = p - PV
                                act.wait_ge(out_ready, o)
                                v = vn[:, j, q * 512:(q + 1) * 512]
                                act.activation(v, main[j][:], ACT.Gelu_apprx_tanh).then_inc(gelu_v, 1)
                                act.wait_ge(gelu_v, g * 8 + (4 * q + j + 1))
                                if q or j:
                                    act.wait_ge(ssv_ready, g * 8 + (4 * q + j))
                                act.activation(junk[:, 0:512], v, ACT.Square, accum_out=ssv[:, j, q:q + 1]).then_inc(ssv_ready, 1)
                            if p in (PU, PU + 1):
                                c = 4 * (p - PU) + j
                                act.wait_ge(out_ready, o)
                                act.activation(uT[:, c, :], main[j][:], ACT.Gelu_apprx_tanh).then_inc(uT_ready, 1)
                            if p in (PGA, PGA + 1):
                                c = 4 * (p - PGA) + j
                                act.wait_ge(out_ready, o)
                                act.activation(sga[:, c, :], main[j][:], ACT.Tanh, scale=0.5).then_inc(tanh_a, 1)
                            if p in (PPA, PPA + 1):
                                round_m(g, 4 * (p - PPA) + j)
                        if p == PK:
                            act.wait_ge(halo_ready, g * 2 + 1)
                            act.wait_ge(ssq_ready, g * 13 + 4)
                            act.activation(sq[:, 0:256], aux[0][:, 0:256], ACT.Square).then_inc(sq_ready, 1)
                        if p == PVA:
                            act.wait_ge(halo_ready, g * 2 + 2)
                            act.activation(va[:, 5, :], aux[1][:, 0:256], ACT.Copy).then_inc(va_done, 1)
                            copy_qT(g, GT - 1)
                    act.wait_ge(out_ready, g * 4 * NP + 4 * NP)

            @block.vector
            def _(dve):
                def split_lo(g, i):
                    _, buf, hi, lo = quarter(i)
                    dve.wait_ge(w_hi_done, g * QPG + (i + 1))
                    dve.tensor_tensor(lo, buf, hi.bitcast(F32), ALU.subtract).then_inc(w_split, 1)

                def prep(n, k):
                    if k < 0:
                        dve.wait_ge(rsx_ready, n + 1)
                        for t in range(GT):
                            dve.tensor_scalar(xn[:, t, :], xn[:, t, :], rsx[:, t:t + 1], None, ALU.mult).then_inc(xn_ready, 1)
                        dve.tensor_scalar(xh, xh, rsx[:, 4:5], None, ALU.mult).then_inc(xn_ready, 1)
                    elif k < KT:
                        dve.wait_ge(hT_hi_done, n * KT + (k + 1))
                        dve.scalar_tensor_tensor(out=hT_lo[:, k, :], in0=aux[k % 4][:], scalar=g_mix[:, k:k + 1],
                                                 in1=hT_hi[:, k, :].bitcast(F32), op0=ALU.mult,
                                                 op1=ALU.subtract).then_inc(hT_done, 1)
                    else:
                        b = k - KT
                        dve.wait_ge(hx_hi_done, n * 2 + (b + 1))
                        for i in range(4):
                            ins = dve.scalar_tensor_tensor(
                                out=hx_lo[:, 4 * b + i, :], in0=aux[b][:, i * P:(i + 1) * P],
                                scalar=g_mix[:, 4 * b + i:4 * b + i + 1], in1=hx_hi[:, 4 * b + i, :].bitcast(F32),
                                op0=ALU.mult, op1=ALU.subtract)
                        ins.then_inc(hx_done, 1)

                dve.sem_inc(x2_done, 8)
                dve.memset(kT[:, :, 0:P], 0.0)
                dve.memset(va[:, 0, :], 0.0).then_inc(halo_kept, 1)
                for i in range(NQ):
                    split_lo(0, i)
                dve.wait_ge(const_in, 96)
                for k in range(-1, KT + 2):
                    prep(0, k)

                def head_norm(g, i, bank, n, gain, dst):
                    h = n // HD
                    dve.wait_ge(sq_ready, g * 13 + (i + 1))
                    dve.reduce_sum(ssq[:, 0:h], sq[:, 0:n].rearrange("p (h d) -> p h d", h=h), AX_X).then_inc(ssq_ready, 1)
                    dve.wait_ge(rsq_ready, g * 13 + (i + 1))
                    for k in range(h):
                        ins = dve.scalar_tensor_tensor(out=dst[:, k, :], in0=bank[:, k * HD:(k + 1) * HD], scalar=rsq[:, k:k + 1],
                                                       in1=gain, op0=ALU.mult, op1=ALU.mult)
                    ins.then_inc(head_normed, 1)

                def rotate(g, t, x):
                    hf = HD // 2
                    r = rot_v.rearrange("p (h d) -> p h d", h=4)
                    cos = rope[:, t, 0, :].unsqueeze(1).to_broadcast([P, 4, hf])
                    sin = rope[:, t, 1, :].unsqueeze(1).to_broadcast([P, 4, hf])
                    x1, x2_ = x[:, :, 0:hf], x[:, :, hf:HD]
                    if t == 0:
                        dve.wait_ge(table_in, g * 32 + 32)
                    dve.wait_ge(head_normed, g * 13 + (9 + t + 1))
                    dve.tensor_tensor(r[:, :, 0:hf], x2_, sin, ALU.mult)
                    dve.tensor_tensor(r[:, :, hf:HD], x1, sin, ALU.mult).then_inc(rope_step, 1)
                    dve.wait_ge(rope_step, g * 2 * GT + (2 * t + 1))
                    dve.tensor_tensor(x1, x1, cos, ALU.mult)
                    dve.tensor_tensor(x2_, x2_, cos, ALU.mult).then_inc(rope_step, 1)
                    dve.wait_ge(rope_step, g * 2 * GT + (2 * t + 2))
                    dve.tensor_tensor(x1, x1, r[:, :, 0:hf], ALU.subtract)
                    dve.tensor_tensor(x2_, x2_, r[:, :, hf:HD], ALU.add).then_inc(q1_roped, 1)
                    dve.wait_ge(q1_roped, g * GT + (t + 1))

                def attend(g, s):
                    if s < NU:
                        n, b = s % GT, s % 2
                        m = 0 if n == 0 else 2 if n == GT - 1 else 1
                        st = stat[:, s % 4, :]
                        dve.wait_ge(s_ps, g * NU + (s + 1))
                        if s == 0:
                            dve.wait_ge(table_in, g * 32 + 32)
                        if s >= 2:
                            dve.wait_ge(exp_done, g * NU + (s - 1))
                        dve.sem_inc(settled, 1)
                        dve.tensor_tensor_reduce(sm[b], aux[b][:, 0:3 * P], mask[:, m, :], 1.0, -BIG, ALU.add, ALU.max,
                                                 st[:, 0:1]).then_inc(s_masked, 1)
                        dve.wait_ge(s_masked, g * NU + (s + 1))
                        dve.tensor_scalar(st[:, 1:2], st[:, 0:1], -SCALE, nsink[:, s // GT:s // GT + 1],
                                          ALU.mult, ALU.min).then_inc(negm_ready, 1)
                    if 0 <= s - 1 < NU:
                        u = s - 1
                        st = stat[:, u % 4, :]
                        dve.wait_ge(exp_done, g * NU + (u + 1))
                        dve.tensor_tensor(st[:, 4:5], st[:, 2:3], st[:, 3:4], ALU.add).then_inc(dve_step, 1)
                        dve.wait_ge(dve_step, g * NU + (u + 1))
                        dve.reciprocal(st[:, 5:6], st[:, 4:5]).then_inc(rden_ready, 1)
                    if 0 <= s - 3 < NU:
                        u = s - 3
                        h, n = divmod(u, GT)
                        dve.wait_ge(o_hi_done, g * NU + (u + 1))
                        dve.tensor_tensor(oT_lo[:, h, n * P:(n + 1) * P], aux[3][:, 0:P],
                                          oT_hi[:, h, n * P:(n + 1) * P].bitcast(F32), ALU.subtract).then_inc(o_done, 1)

                def mixed(g, c):
                    dve.wait_ge(sp_ps, g * KT + (c + 1))
                    if c == 0:
                        dve.wait_ge(bsp_in, g * 16 + 16)
                    if c >= 2:
                        dve.wait_ge(a_done, g * KT + (c - 1))
                    dve.scalar_tensor_tensor(out=tmp[c % 2].rearrange("p (n q) -> p n q", n=GT),
                                             in0=aux[c % 4][:].rearrange("p (n q) -> p n q", n=GT),
                                             scalar=g_v[:, c:c + 1],
                                             in1=bsp[:, c, :].unsqueeze(1).to_broadcast([P, GT, P]),
                                             op0=ALU.mult, op1=ALU.add).then_inc(mixed_ready, 1)

                def a_lo(g, c):
                    dve.wait_ge(a_hi_done, g * KT + (c + 1))
                    dve.tensor_tensor(aT_lo[:, c, :], tmp[c % 2], aT_hi[:, c, :].bitcast(F32),
                                      ALU.subtract).then_inc(a_done, 1)

                with dve.Fori(0, NG) as g:
                    for p in range(NP):
                        if p == PU:
                            dve.wait_ge(rsv_ready, g + 1)
                            for t in range(GT):
                                dve.tensor_scalar(vn[:, t, :], vn[:, t, :], rsv[:, t:t + 1], None, ALU.mult).then_inc(vn_ready, 1)
                        for j in range(4):
                            for q in SPLIT_AT[p][j]:
                                split_lo(g, NQ * (p + 1) + q)
                            if p == POUT and j == 3:
                                prep(g + 1, -1)
                            o = g * 4 * NP + (4 * p + j + 1)
                            if p in (PGB, PGB + 1):
                                for s in slots_of(4 * (p - PGB) + j):
                                    attend(g, s)
                            if p == PU + 1:
                                mixed(g, j)
                                a_lo(g, j)
                            if p == PGA:
                                mixed(g, 4 + j)
                                a_lo(g, 4 + j)
                            if p == POUT + 1 and j:
                                for k in PREP_AT[j]:
                                    prep(g + 1, k)
                                if j == 3:
                                    prep(g + 1, KT)
                                    prep(g + 1, KT + 1)
                            if p == PK:
                                head_norm(g, j, main[j], 256, gk, kn[:, j, :].rearrange("p (h d) -> p h d", h=2))
                            if p in (PQ, PQ + 1):
                                heads = qn[:, p - PQ, j, :].rearrange("p (h d) -> p h d", h=4)
                                head_norm(g, 5 + 4 * (p - PQ) + j, main[j], 512, gq, heads)
                                if p == PQ + 1:
                                    rotate(g, j, heads)
                            if p in (PPB, PPB + 1):
                                c = 4 * (p - PPB) + j
                                dve.wait_ge(out_ready, o)
                                dve.wait_ge(sgb_ready, g * KT + (c + 1))
                                dve.tensor_tensor(sgb[:, c, :], main[j][:], sgb[:, c, :], ALU.mult).then_inc(mb_done, 1)
                            if p in (PPA, PPA + 1):
                                c = 4 * (p - PPA) + j
                                dve.wait_ge(out_ready, o)
                                dve.wait_ge(sga_ready, g * KT + (c + 1))
                                if c >= 2:
                                    dve.wait_ge(m_done, g * KT + (c - 1))
                                dve.tensor_tensor(tmp[c % 2], main[j][:], sga[:, c, :], ALU.mult).then_inc(ya_gated, 1)
                                dve.wait_ge(m_hi_done, g * KT + (c + 1))
                                dve.tensor_tensor(m_lo[:, c, :], tmp[c % 2], m_hi[:, c, :].bitcast(F32),
                                                  ALU.subtract).then_inc(m_done, 1)
                            if p >= POUT:
                                q = p - POUT
                                dve.wait_ge(out_ready, o)
                                if j == 0:
                                    dve.wait_ge(x2_in[q], g * 16 + 16)
                                r = x2[:, j, q * 512:(q + 1) * 512]
                                dve.tensor_tensor(r, main[j][:], r, ALU.add).then_inc(x2_done, 1)
                        if p == PK:
                            head_norm(g, 4, aux[0], 256, gk, kn[:, 4, :].rearrange("p (h d) -> p h d", h=2))

            @block.gpsimd
            def _(pool):
                def settle():
                    pool.sem_inc(settled, 1)

                def rms(out, ss, n, width, link):
                    settle()
                    pool.tensor_scalar(out, ss, 1.0 / width, EPS, ALU.mult, ALU.add).then_inc(pool_step, 1)
                    pool.wait_ge(pool_step, link())
                    return pool.tensor_tensor(out, out, half[:, 0:n], ALU.pow)

                counted = {"n": 0, "per": 0}

                def link_at(g, base):
                    def link():
                        counted["n"] += 1
                        return g * PER_BODY + (base + counted["n"])
                    return link

                PREP_STEPS = 1
                PER_BODY = 13 + 9 * 2 + 2 + 1

                def load_x(row, halo):
                    pool.dma_start(xn, a["x_all"][bass.ds(row, G), :].rearrange("(t p) d -> p t d", p=P)).then_inc(x_in, 16)
                    pool.dma_start(xh, a["x_all"][bass.ds(halo, P), :]).then_inc(xh_in, 16)

                def load_tables(n):
                    pool.dma_start(rope, a["rope"][bass.ds(n * P, P), :].rearrange("p (t c f) -> p t c f", t=5, c=2)).then_inc(table_in, 16)
                    pool.dma_start(mask, a["mask"][bass.ds(n * P, P), :].rearrange("p (m k) -> p m k", m=3)).then_inc(table_in, 16)

                load_x(0, G)
                pool.dma_start(ws, a["w_spatial"].rearrange("g p q -> p g q")).then_inc(ws_in, 16)
                pool.memset(half, -0.5).then_inc(const_set, 1)
                pool.wait_ge(const_set, 1)
                load_tables(0)
                pool.wait_ge(ssx_ready, 5)
                rms(rsx[:, 0:5], ssx[:, 0:5], 5, D, link_at(0, 0)).then_inc(rsx_ready, 1)
                counted["n"] = 0
                pool.wait_ge(const_in, 96)

                with pool.Fori(0, NG) as g:
                    link = link_at(g, PREP_STEPS)

                    def head_rms(i, h):
                        pool.wait_ge(ssq_ready, g * 13 + (i + 1))
                        rms(rsq[:, 0:h], ssq[:, 0:h], h, HD, link).then_inc(rsq_ready, 1)

                    def rotate(i, t, h, dst):
                        n = h * HD
                        pool.wait_ge(head_normed, g * 13 + (i + 1))
                        x = dst.rearrange("p (h d) -> p h d", h=h)
                        r = rot[:, 0:n].rearrange("p (h d) -> p h d", h=h)
                        hf = HD // 2
                        cos = rope[:, t, 0, :].unsqueeze(1).to_broadcast([P, h, hf])
                        sin = rope[:, t, 1, :].unsqueeze(1).to_broadcast([P, h, hf])
                        x1, x2_ = x[:, :, 0:hf], x[:, :, hf:HD]
                        pool.tensor_tensor(r[:, :, 0:hf], x2_, sin, ALU.mult)
                        pool.tensor_tensor(r[:, :, hf:HD], x1, sin, ALU.mult).then_inc(pool_step, 1)
                        pool.wait_ge(pool_step, link())
                        pool.tensor_tensor(x1, x1, cos, ALU.mult)
                        pool.tensor_tensor(x2_, x2_, cos, ALU.mult).then_inc(pool_step, 1)
                        pool.wait_ge(pool_step, link())
                        pool.tensor_tensor(x1, x1, r[:, :, 0:hf], ALU.subtract)
                        pool.tensor_tensor(x2_, x2_, r[:, :, hf:HD], ALU.add).then_inc(head_roped, 1)
                        pool.wait_ge(head_roped, g * 9 + (i + 1))

                    def weigh(s):
                        if 0 <= s < NU:
                            pool.wait_ge(rden_ready, g * NU + (s + 1))
                            settle()
                            pool.tensor_scalar(pr[s % 3], pr[s % 3], stat[:, s % 4, 5:6], 1.0, ALU.mult,
                                               ALU.mult).then_inc(p_ready, 1)

                    pool.wait_ge(table_in, g * 32 + 32)
                    for t in range(5):
                        head_rms(t, NKV)
                    for t in range(5):
                        rotate(t, t, NKV, kn[:, t, :])
                        if t == 3:
                            head_rms(5, 4)
                    for t in range(GT):
                        head_rms(5 + t + 1, 4)
                        rotate(5 + t, t, 4, qn[:, 0, t, :])
                    for i in range(1 + GT, 2 * GT):
                        head_rms(5 + i, 4)
                    for c in range(KT):
                        for s in slots_of(c):
                            weigh(s - 1)
                        pool.wait_ge(tanh_b, g * KT + (c + 1))
                        settle()
                        pool.tensor_scalar(sgb[:, c, :], sgb[:, c, :], 0.5, 0.5, ALU.mult, ALU.add).then_inc(sgb_ready, 1)
                    pool.wait_ge(o_ps, g * NU + NU)
                    settle()
                    pool.tensor_copy(kT[:, :, 0:P], kT[:, :, GT * P:(GT + 1) * P])
                    pool.tensor_copy(va[:, 0, :], va[:, GT, :]).then_inc(halo_kept, 1)
                    pool.dma_start(bsp, a["b_spatial"].to_broadcast([P, NH * P]).rearrange("p (g q) -> p g q", g=NH)).then_inc(bsp_in, 16)
                    pool.wait_ge(ssv_ready, g * 8 + 8)
                    pool.tensor_tensor(rsv, ssv[:, :, 0], ssv[:, :, 1], ALU.add).then_inc(pool_step, 1)
                    pool.wait_ge(pool_step, link())
                    rms(rsv, rsv, GT, D, link).then_inc(rsv_ready, 1)
                    for c in range(KT):
                        pool.wait_ge(mixed_ready, g * KT + (c + 1))
                        pool.wait_ge(uT_ready, g * KT + (c + 1))
                        pool.tensor_tensor(tmp[c % 2], tmp[c % 2], uT[:, c, :], ALU.mult).then_inc(a_ready, 1)
                        if c >= 4:
                            pool.wait_ge(tanh_a, g * KT + (c - 3))
                            settle()
                            pool.tensor_scalar(sga[:, c - 4, :], sga[:, c - 4, :], 0.5, 0.5, ALU.mult, ALU.add).then_inc(sga_ready, 1)
                    for c in range(4, KT):
                        pool.wait_ge(tanh_a, g * KT + (c + 1))
                        settle()
                        pool.tensor_scalar(sga[:, c, :], sga[:, c, :], 0.5, 0.5, ALU.mult, ALU.add).then_inc(sga_ready, 1)
                    for c in range(KT):
                        pool.wait_ge(ya_gated, g * KT + (c + 1))
                        pool.tensor_tensor(tmp[c % 2], tmp[c % 2], sgb[:, c, :], ALU.add).then_inc(m_ready, 1)
                    pool.wait_ge(out_ready, g * 4 * NP + 4 * (PPA + 2))
                    pool.wait_ge(m_done, g * KT + KT)
                    settle()
                    load_x(g * G + G, g * G + 2 * G)
                    for q in range(2):
                        pool.dma_start(x2[:, :, q * 512:(q + 1) * 512],
                                       a["x_all"][bass.ds(g * G, G), q * 512:(q + 1) * 512].rearrange("(t p) d -> p t d", p=P)).then_inc(x2_in[q], 16)
                    load_tables(g + 1)
                    pool.wait_ge(ssx_ready, g * 5 + 10)
                    rms(rsx[:, 0:5], ssx[:, 0:5], 5, D, link).then_inc(rsx_ready, 1)
                    for t in range(GT):
                        pool.wait_ge(x2_done, g * 8 + (8 + 4 + t + 1))
                        settle()
                        for dst in (a["y"], a["x2s"]):
                            pool.dma_start(dst[bass.ds(g * G + t * P, P), :], x2[:, t, :]).then_inc(y_out, 16)
                    pool.wait_ge(y_out, g * 2 * GT * 16 + 2 * GT * 16)
                assert counted["n"] == PER_BODY, counted


def route(nc, a, held):
    with ExitStack() as ctx:
        def sb(name, shape, dt=F32):
            return ctx.enter_context(nc.sbuf_tensor(name, shape, dt))[...]

        def sem(name):
            return ctx.enter_context(nc.semaphore(name))

        NR = N_GROUPS + NE
        NX = NT // 2
        x = sb("r_x", [P, NT, D])
        junk = sb("r_junk", [P, D])
        xT = sb("r_xT", [P, 4, KT, P])
        w_r = sb("r_w", [P, KT, NR])
        bias = sb("r_bias", [P, NR])
        g_ffn, ident = held["g_ffn"], held["ident"]
        upper, ones = sb("r_upper", [P, P]), sb("r_ones", [P, P])
        cst = sb("r_cst", [P, 2, EPG])
        row = sb("r_row", [P, P])
        ids, pad_id = sb("r_ids", [P, NT]), sb("r_pad_id", [P, 1])
        zero = sb("r_zero", [P, D])
        half = sb("r_half", [P, GT])
        ss, rs = sb("r_ss", [P, NT]), sb("r_rs", [P, NT])
        logits = sb("r_logits", [P, NT, NR])
        gmax, gsum, gp = sb("r_gmax", [P, NT]), sb("r_gsum", [P, NT]), sb("r_gp", [P, NT])
        s4, eg, ohg = sb("r_s4", [P, NT, N_GROUPS]), sb("r_eg", [P, NT, N_GROUPS]), sb("r_ohg", [P, NT, N_GROUPS])
        pick = sb("r_pick", [P, NT])
        prod = sb("r_prod", [P, NT, NE])
        esel, s8 = sb("r_esel", [P, NT, EPG]), sb("r_s8", [P, NT, EPG])
        oh = [sb(f"r_oh{k}", [P, NT, EPG]) for k in range(2)]
        m = [sb(f"r_m{k}", [P, NT]) for k in range(2)]
        dif, ratio, den = sb("r_dif", [P, NT]), sb("r_ratio", [P, NT]), sb("r_den", [P, NT])
        A = [sb(f"r_A{k}", [P, NT, NE]) for k in range(2)]
        Asum = sb("r_Asum", [P, NT, NE])
        cum = sb("r_cum", [P, NT + 1, NE])
        pos = sb("r_pos", [P, NT, NE])
        gate, value = sb("r_gate", [P, 2, NT]), sb("r_value", [P, 2, NT])
        dest_f, dest = sb("r_dest_f", [P, 2, NT]), sb("r_dest", [P, 2, NT], I32)
        part_i, blk_i = sb("r_part_i", [P, 2, NT], I32), sb("r_blk_i", [P, 2, NT], I32)
        part, blk = sb("r_part", [P, 2, NT]), sb("r_blk", [P, 2, NT])
        in_part = sb("r_in_part", [P, 2 * NT, P])
        in_blk = sb("r_in_blk", [P, 2 * NT, NTAB])
        carried = sb("r_carried", [P, 2 * NT, 2, NTAB])
        nb_i, nb = sb("r_nb_i", [P, NE], I32), sb("r_nb", [P, NE])
        pend, first = sb("r_pend", [P, NE]), sb("r_first", [P, NE])
        onesr = sb("r_onesr", [P, NE])
        before, starts = sb("r_before", [P, NE]), sb("r_starts", [P, NE])
        be, bs, is_first = sb("r_be", [P, 1]), sb("r_bs", [P, 1]), sb("r_is_first", [P, 1])
        tabT = sb("r_tabT", [P, TW], I32)

        bank = [ctx.enter_context(nc.psum_tensor(f"r_ps{i}", [P, 512], F32)) for i in range(8)]
        ident_in, wr_in, const_in, x_in, zero_set, set_done, wr_done, pads_out = (
            sem("r_ident_in"), sem("r_wr_in"), sem("r_const_in"), [sem(f"r_x_in{i}") for i in range(NX)], sem("r_zero_set"),
            sem("r_set_done"), sem("r_wr_done"), sem("r_pads_out"))
        sq_done, rs_done, x_ps, xT_act, xT_dve, l_ps = (
            sem("r_sq_done"), sem("r_rs_done"), sem("r_x_ps"), sem("r_xT_act"), sem("r_xT_dve"), sem("r_l_ps"))
        gsub_ready, eg_done, dif_ready, ratio_done, A_ready, rank_ps = (
            sem("r_gsub_ready"), sem("r_eg_done"), sem("r_dif_ready"), sem("r_ratio_done"), sem("r_A_ready"), sem("r_rank_ps"))
        step, pstep, half_ready, carried_ready, part_ready, slots_ps, tab_ready, tab_out = (
            sem("r_step"), sem("r_pstep"), sem("r_half_ready"), sem("r_carried_ready"), sem("r_part_ready"),
            sem("r_slots_ps"), sem("r_tab_ready"), sem("r_tab_out"))

        with nc.Block() as block:

            @block.sync
            def _(sp):
                def load_x(i):
                    sp.dma_start(x[:, 2 * i:2 * i + 2, :],
                                 a["x2s"][2 * i * P:(2 * i + 2) * P, :].rearrange("(t p) d -> p t d", p=P)).then_inc(x_in[i], 16)

                sp.dma_start(ident, a["ident"]).then_inc(ident_in, 16)
                load_x(0)
                sp.dma_start(g_ffn, a["norm_ffn_g"]).then_inc(wr_in, 16)
                sp.dma_start(w_r[:, :, 0:N_GROUPS], a["w_router_group"].rearrange("(k p) c -> p k c", p=P)).then_inc(wr_in, 16)
                sp.dma_start(w_r[:, :, N_GROUPS:], a["w_router_expert"].rearrange("(k p) c -> p k c", p=P)).then_inc(wr_in, 16)
                load_x(1)
                sp.dma_start(bias[:, 0:N_GROUPS], a["b_router_group"].to_broadcast([P, N_GROUPS])).then_inc(const_in, 16)
                sp.dma_start(bias[:, N_GROUPS:], a["b_router_expert"].to_broadcast([P, NE])).then_inc(const_in, 16)
                for i in range(2, NX):
                    load_x(i)
                sp.dma_start(upper, a["upper"]).then_inc(const_in, 16)
                sp.dma_start(cst, a["counts"].to_broadcast([P, 2 * EPG]).rearrange("p (a b) -> p a b", a=2)).then_inc(const_in, 16)
                sp.dma_start(row, a["row"].to_broadcast([P, P])).then_inc(const_in, 16)
                sp.dma_start(ids, a["ids"]).then_inc(const_in, 16)
                sp.wait_ge(zero_set, 1)
                for dst in (a["y"], a["x2s"]):
                    sp.dma_start(dst[T:T + P, :], zero).then_inc(pads_out, 16)
                sp.wait_ge(tab_ready, 1)
                sp.dma_start(a["table"].rearrange("o (n c) -> (o n) c", c=TW), tabT[0:NTAB, :]).then_inc(tab_out, 16)
                sp.wait_ge(tab_out, 16)
                sp.dma_start(held["tab"], a["table"]).then_inc(held["tab_in"], 16)
                sp.wait_ge(held["tab_in"], 16)
                e = sp.value_load(held["tab"][0:1, 0:1], min_val=0, max_val=NE - 1)
                for w in ("g", "u"):
                    for h in range(2):
                        load_weights(sp, a, held, w, h, e)
                sp.wait_ge(pads_out, 32)

            @block.tensor
            def _(pe):
                def turn(t):
                    pe.wait_ge(x_in[t // 2], 16)
                    for b in range(2):
                        if t >= 2:
                            pe.wait_ge((xT_act, xT_dve)[b], t - 1)
                        ps = bank[2 * (t % 2) + b]
                        for k in range(4):
                            c = (4 * b + k) * P
                            mm = pe.transpose(ps[:, k * P:(k + 1) * P], x[:, t, c:c + P], ident)
                        mm.then_inc(x_ps, 1)

                def product(t):
                    for k in range(KT):
                        if k % 4 == 0:
                            pe.wait_ge((xT_act, xT_dve)[k // 4], t + 1)
                        c = 64 * (t % GT)
                        mm = pe.matmul(bank[4 + t // GT][:, c:c + NR], xT[:, t % 4, k, :], w_r[:, k, :],
                                       start=(k == 0), stop=(k == KT - 1))
                    mm.then_inc(l_ps, 1)

                pe.wait_ge(ident_in, 16)
                turn(0)
                pe.wait_ge(wr_done, 1)
                for t in range(NT):
                    if t + 1 < NT:
                        turn(t + 1)
                    product(t)
                pe.wait_ge(A_ready, 1)
                pe.wait_ge(set_done, 1)
                pe.wait_ge(const_in, 6 * 16)
                flat = Asum.rearrange("p t e -> p (t e)")
                pe.matmul(bank[1][:, 0:NT * NE], ones, flat, start=True, stop=True).then_inc(rank_ps, 1)
                pe.matmul(bank[0][:, 0:NT * NE], upper, flat, start=True, stop=True).then_inc(rank_ps, 1)
                pe.wait_ge(carried_ready, 2)
                for i in range(2 * NT):
                    pe.wait_ge(part_ready, i + 1)
                    mm = pe.matmul(bank[2][:, 0:2 * NTAB], in_part[:, i, :], carried[:, i, :, :].rearrange("p c b -> p (c b)"),
                                   start=(i == 0), stop=(i == 2 * NT - 1))
                mm.then_inc(slots_ps, 1)

            @block.scalar
            def _(act):
                for t in range(NT):
                    act.wait_ge(x_ps, 2 * t + 1)
                    if t >= 4:
                        act.wait_ge(l_ps, t - 3)
                    act.activation(xT[:, t % 4, 0:4, :], bank[2 * (t % 2)][:].rearrange("p (k q) -> p k q", k=4),
                                   ACT.Copy).then_inc(xT_act, 1)
                    if t:
                        act.wait_ge(sq_done, t)
                    act.activation(junk, x[:, t, :], ACT.Square, accum_out=ss[:, t:t + 1]).then_inc(sq_done, 1)
                act.wait_ge(gsub_ready, 1)
                act.activation(eg, s4, ACT.Exp).then_inc(eg_done, 1)
                act.wait_ge(dif_ready, 1)
                act.activation(ratio, dif, ACT.Exp).then_inc(ratio_done, 1)

            @block.vector
            def _(dve):
                n = [0]

                def link(ins):
                    n[0] += 1
                    ins.then_inc(step, 1)
                    dve.wait_ge(step, n[0])

                def over(ap, n_):
                    return ap.unsqueeze(2).to_broadcast([P, NT, n_])

                def across(ap):
                    return ap.unsqueeze(1).to_broadcast([P, NT, ap.shape[-1]])

                dve.memset(zero, 0.0).then_inc(zero_set, 1)
                dve.memset(onesr, 1.0)
                dve.memset(cum[:, 0, :], 0.0)
                dve.memset(ones, 1.0).then_inc(set_done, 1)
                dve.wait_ge(set_done, 1)
                for t in range(NT):
                    if t == 1:
                        dve.wait_ge(wr_in, 3 * 16)
                        dve.tensor_tensor(w_r, w_r, g_ffn.unsqueeze(2).to_broadcast([P, KT, NR]), ALU.mult).then_inc(wr_done, 1)
                    dve.wait_ge(x_ps, 2 * t + 2)
                    if t >= 4:
                        dve.wait_ge(l_ps, t - 3)
                    dve.tensor_copy(xT[:, t % 4, 4:8, :], bank[2 * (t % 2) + 1][:].rearrange("p (k q) -> p k q", k=4)).then_inc(xT_dve, 1)
                dve.wait_ge(const_in, 6 * 16)
                link(dve.tensor_scalar(pad_id, ids[:, 0:1], float(T), None, ALU.add))
                for r in range(NG):
                    dve.wait_ge(rs_done, r + 1)
                    dve.wait_ge(l_ps, (r + 1) * GT)
                    for i in range(GT):
                        t = r * GT + i
                        ins = dve.scalar_tensor_tensor(out=logits[:, t, :], in0=bank[4 + r][:, 64 * i:64 * i + NR],
                                                       scalar=rs[:, t:t + 1], in1=bias, op0=ALU.mult, op1=ALU.add)
                link(ins)

                gl, el = logits[:, :, 0:N_GROUPS], logits[:, :, N_GROUPS:]

                def first_max(vals, width, top, scratch, onehot):
                    link(dve.tensor_reduce(top, vals, AX_X, ALU.max))
                    link(dve.tensor_tensor(scratch, vals, over(top, width), ALU.is_equal))
                    link(dve.scalar_tensor_tensor(out=scratch, in0=scratch, scalar=-100.0, in1=across(cst[:, 0, 0:width]),
                                                  op0=ALU.mult, op1=ALU.add))
                    link(dve.tensor_reduce(pick, scratch, AX_X, ALU.min))
                    link(dve.tensor_tensor(onehot, across(cst[:, 1, 0:width]), over(pick, width), ALU.is_equal))

                first_max(gl, N_GROUPS, gmax, s4, ohg)
                dve.tensor_tensor(s4, gl, over(gmax, N_GROUPS), ALU.subtract).then_inc(gsub_ready, 1)
                p4 = prod.rearrange("p t (g e) -> p t g e", g=N_GROUPS)
                link(dve.tensor_tensor(p4, el.rearrange("p t (g e) -> p t g e", g=N_GROUPS),
                                       ohg.unsqueeze(3).to_broadcast([P, NT, N_GROUPS, EPG]), ALU.mult))
                link(dve.reduce_sum(esel, prod.rearrange("p t (g e) -> p t e g", g=N_GROUPS), AX_X))
                first_max(esel, EPG, m[0], s8, oh[0])
                link(dve.scalar_tensor_tensor(out=esel, in0=oh[0], scalar=-BIG, in1=esel, op0=ALU.mult, op1=ALU.add))
                first_max(esel, EPG, m[1], s8, oh[1])
                dve.tensor_tensor(dif, m[1], m[0], ALU.subtract).then_inc(dif_ready, 1)
                for k in range(2):
                    link(dve.tensor_tensor(A[k].rearrange("p t (g e) -> p t g e", g=N_GROUPS),
                                           ohg.unsqueeze(3).to_broadcast([P, NT, N_GROUPS, EPG]),
                                           oh[k].unsqueeze(2).to_broadcast([P, NT, N_GROUPS, EPG]), ALU.mult))
                link(dve.tensor_tensor(Asum, A[0], A[1], ALU.add))
                dve.sem_inc(A_ready, 1)
                dve.wait_ge(eg_done, 1)
                link(dve.reduce_sum(gsum, eg, AX_X))
                link(dve.reciprocal(gp, gsum))
                dve.wait_ge(ratio_done, 1)
                link(dve.tensor_scalar(den, ratio, 1.0, None, ALU.add))
                link(dve.reciprocal(den, den))
                link(dve.tensor_tensor(gate[:, 0, :], gp, den, ALU.mult))
                link(dve.tensor_tensor(gate[:, 1, :], gate[:, 0, :], ratio, ALU.mult))
                dve.wait_ge(rank_ps, 1)
                for t in range(NT):
                    link(dve.tensor_tensor(cum[:, t + 1, :], bank[1][:, t * NE:(t + 1) * NE], cum[:, t, :], ALU.add))
                link(dve.tensor_scalar(nb_i, cum[:, NT, :], float(P - 1), None, ALU.add))
                link(dve.tensor_scalar(nb_i, nb_i, 7, None, ALU.arith_shift_right))
                link(dve.tensor_copy(nb, nb_i))
                link(dve.tensor_tensor_scan(pend, onesr, nb, 0.0, ALU.mult, ALU.add))
                link(dve.tensor_scalar(before, pend, ids[:, 0:1], None, ALU.is_le))
                link(dve.reduce_sum(be, before, AX_X))
                link(dve.tensor_tensor(starts, before, pend, ALU.mult))
                link(dve.tensor_reduce(bs, starts, AX_X, ALU.max))
                dve.tensor_scalar(tabT[:, 0:1], be, float(NE - 1), None, ALU.min)
                link(dve.tensor_tensor(is_first, bs, ids[:, 0:1], ALU.is_equal))
                dve.scalar_tensor_tensor(out=tabT[:, 1:2], in0=pend[:, NE - 1:NE], scalar=ids[:, 0:1], in1=is_first,
                                         op0=ALU.is_gt, op1=ALU.mult)
                link(dve.tensor_copy(tabT[:, 2:3], pend[:, NE - 1:NE]))
                dve.sem_inc(tab_ready, 1)
                link(dve.tensor_tensor(first, pend, nb, ALU.subtract))
                dve.wait_ge(rank_ps, 2)
                link(dve.tensor_tensor(pos, bank[0][:, 0:NT * NE].rearrange("p (t e) -> p t e", t=NT), cum[:, 0:NT, :], ALU.add))
                link(dve.scalar_tensor_tensor(out=pos, in0=across(first), scalar=float(P), in1=pos, op0=ALU.mult, op1=ALU.add))
                for k in range(2):
                    link(dve.tensor_tensor(prod, A[k], pos, ALU.mult))
                    link(dve.reduce_sum(dest_f[:, k, :], prod, AX_X))
                link(dve.tensor_copy(dest, dest_f))
                dve.tensor_scalar(part_i, dest, P - 1, None, ALU.bitwise_and)
                link(dve.tensor_scalar(blk_i, dest, 7, None, ALU.arith_shift_right))
                dve.tensor_copy(blk, blk_i)
                link(dve.tensor_copy(part, part_i))
                link(dve.tensor_tensor(value, ids.unsqueeze(1).to_broadcast([P, 2, NT]), part, ALU.subtract))
                link(dve.tensor_scalar(value, value, float(-T), None, ALU.add))
                link(dve.tensor_tensor(in_blk, blk.rearrange("p k t -> p (k t)").unsqueeze(2).to_broadcast([P, 2 * NT, NTAB]),
                                       row[:, 0:NTAB].unsqueeze(1).to_broadcast([P, 2 * NT, NTAB]), ALU.is_equal))
                for c, what in ((0, value), (1, gate)):
                    dve.tensor_tensor(carried[:, :, c, :], in_blk,
                                      what.rearrange("p k t -> p (k t)").unsqueeze(2).to_broadcast([P, 2 * NT, NTAB]),
                                      ALU.mult).then_inc(carried_ready, 1)
                for i in range(2 * NT):
                    dve.tensor_scalar(in_part[:, i, :], row, part.rearrange("p k t -> p (k t)")[:, i:i + 1], None,
                                      ALU.is_equal).then_inc(part_ready, 1)
                dve.wait_ge(slots_ps, 1)
                dve.tensor_scalar(held["slots"][:, :, 0].bitcast(I32), bank[2][:, 0:NTAB], pad_id, None, ALU.add)
                dve.tensor_copy(held["slots"][:, :, 1], bank[2][:, NTAB:2 * NTAB])

            @block.gpsimd
            def _(pool):
                pool.memset(half, -0.5).then_inc(half_ready, 1)
                pool.wait_ge(half_ready, 1)
                for r in range(NG):
                    pool.wait_ge(sq_done, (r + 1) * GT)
                    tiles = slice(r * GT, (r + 1) * GT)
                    pool.tensor_scalar(rs[:, tiles], ss[:, tiles], 1.0 / D, EPS, ALU.mult, ALU.add).then_inc(pstep, 1)
                    pool.wait_ge(pstep, r + 1)
                    pool.tensor_tensor(rs[:, tiles], rs[:, tiles], half, ALU.pow).then_inc(rs_done, 1)


def load_weights(sp, a, held, w, h, e, new=None):
    dst, name = held["w" + w], {"g": "w_gate_e", "u": "w_up_e", "d": "w_down_e"}[w]
    k = dst.shape[1] // 2
    src = a[name][bass.ds(e, 1), h * k * P:(h + 1) * k * P, :].rearrange("o (k p) c -> p (o k) c", p=P)
    sp.dma_start(dst[:, h * k:(h + 1) * k, :], src, cond=new, bounds_check=None).then_inc(held[f"w{w}_in"][h], 16)


def lo_splitter(eng, raw, hi, lo, hi_done, lo_done):
    def split_lo(i, w, h):
        eng.wait_ge(hi_done[w], i * 2 + (h + 1))
        half = slice(4 * h, 4 * h + 4)
        eng.tensor_tensor(lo[w][:, half, :], raw[w][:, half, :], hi[w][:, half, :].bitcast(F32), ALU.subtract).then_inc(lo_done[w], 1)
    return split_lo


def experts(nc, a, held):
    with ExitStack() as ctx:
        def sb(name, shape, dt=F32):
            return ctx.enter_context(nc.sbuf_tensor(name, shape, dt))[...]

        def sem(name):
            return ctx.enter_context(nc.semaphore(name))

        wg, wu, wd, tab, slots = (held[name] for name in ("wg", "wu", "wd", "tab", "slots"))
        ident, g_ffn, half = held["ident"], held["g_ffn"], sb("e_half", [P, 1])
        nxt, prv = sb("e_nxt", [P, 2]), sb("e_prv", [P, 2])
        xg, junk = sb("e_xg", [P, D]), sb("e_junk", [P, D])
        ss, ms, rs, hrs, hrs2 = (sb(f"e_{n}", [P, 1]) for n in ("ss", "ms", "rs", "hrs", "hrs2"))
        xT, xT_hi, xT_lo = sb("e_xT", [P, KT, P]), sb("e_xT_hi", [P, KT, P], F32R), sb("e_xT_lo", [P, KT, P], F32R)
        raw = {"g": wg, "u": wu}
        hi, lo = ({w: sb(f"e_{w}_{part}", [P, KT, DE], F32R) for w in "gu"} for part in ("hi", "lo"))
        th, hid, hidT = sb("e_th", [P, DE]), sb("e_hid", [P, DE]), sb("e_hidT", [P, DE // P, P])
        yo = sb("e_yo", [P, D])
        ps_g, ps_u, ps_h = (ctx.enter_context(nc.psum_tensor(f"e_ps{n}", [P, 512], F32)) for n in "guh")
        ps_x = [ctx.enter_context(nc.psum_tensor(f"e_psx{i}", [P, 512], F32)) for i in range(2)]
        ps_y = [ctx.enter_context(nc.psum_tensor(f"e_psy{i}", [P, 512], F32)) for i in range(2)]

        tab_in, wg_in, wu_in, wd_in = (held[name] for name in ("tab_in", "wg_in", "wu_in", "wd_in"))
        hi_done, lo_done = ({w: sem(f"e_{w}_{part}_done") for w in "gu"} for part in ("hi", "lo"))
        x_hi_done, x_lo_done = sem("e_x_hi_done"), sem("e_x_lo_done")
        w_in = {"g": wg_in, "u": wu_in}
        set_done, x_in, y_out = sem("e_set_done"), sem("e_x_in"), sem("e_y_out")
        g_ps, u_ps, x_ps, y_ps, h_ps = sem("e_g_ps"), sem("e_u_ps"), sem("e_x_ps"), sem("e_y_ps"), sem("e_h_ps")
        xT_done, tanh_done, glu_done, hid_done, hidT_done, yo_done = (
            sem("e_xT_done"), sem("e_tanh_done"), sem("e_glu_done"), sem("e_hid_done"), sem("e_hidT_done"), sem("e_yo_done"))
        ss_done, rs_done, shifted, pstep, settled = (
            sem("e_ss_done"), sem("e_rs_done"), sem("e_shifted"), sem("e_pstep"), sem("e_settled"))

        with nc.Block() as block:

            def blocks(eng):
                eng.wait_ge(tab_in, 16)
                return eng.value_load(tab[0:1, 2:3], min_val=2 * T // P, max_val=MAXB)

            @block.sync
            def _(sp):
                n = blocks(sp)

                def load(i, w, h, free=None, count=None):
                    e = sp.value_load(tab[0:1, bass.ds(i * TW, 1)], min_val=0, max_val=NE - 1)
                    new = sp.value_load(tab[0:1, bass.ds(i * TW + 1, 1)], min_val=0, max_val=1)
                    if free is not None:
                        sp.wait_ge(free, count)
                        sp.sem_inc(settled, 1)
                    load_weights(sp, a, held, w, h, e, new)

                sp.wait_ge(x_in, 16)
                for h in range(2):
                    load(1, "g", h, lo_done["g"], h + 1)
                for h in range(2):
                    load(0, "d", h)
                for h in range(2):
                    load(1, "u", h, lo_done["u"], h + 1)
                for h, w in ((0, "g"), (0, "u"), (1, "g"), (1, "u")):
                    load(2, w, h, lo_done[w], h + 3)
                with sp.Fori(1, n) as i:
                    load(i + 2, "g", 0, lo_done["g"], i * 2 + 3)
                    load(i, "d", 0, y_ps, i * 2 + 3)
                    load(i + 2, "u", 0, lo_done["u"], i * 2 + 3)
                    load(i + 2, "g", 1, lo_done["g"], i * 2 + 4)
                    load(i, "d", 1, y_ps, i * 2 + 4)
                    load(i + 2, "u", 1, lo_done["u"], i * 2 + 4)
                for done in wg_in + wu_in:
                    sp.wait_ge(done, n * 16 + 32)
                    sp.sem_inc(settled, 1)

            @block.tensor
            def _(pe):
                n = blocks(pe)

                def turn_x(i):
                    pe.wait_ge(x_in, (i + 1) * 16)
                    for b in range(2):
                        for k in range(4):
                            c = (4 * b + k) * P
                            mm = pe.transpose(ps_x[b][:, k * P:(k + 1) * P], xg[:, c:c + P], ident)
                        mm.then_inc(x_ps, 1)

                def gate_up(i):
                    pe.wait_ge(x_lo_done, i + 1)
                    for w, ps, done in (("g", ps_g, g_ps), ("u", ps_u, u_ps)):
                        for k in range(KT):
                            if k % 4 == 0:
                                pe.wait_ge(lo_done[w], i * 2 + (k // 4 + 1))
                            pe.matmul(ps[:], xT_hi[:, k, :], hi[w][:, k, :], start=(k == 0), stop=False)
                            pe.matmul(ps[:], xT_hi[:, k, :], lo[w][:, k, :], start=False, stop=False)
                            mm = pe.matmul(ps[:], xT_lo[:, k, :], hi[w][:, k, :], start=False, stop=(k == KT - 1))
                            if k % 4 == 3:
                                mm.then_inc(done, 1)

                def down(i):
                    pe.wait_ge(hidT_done, i + 1)
                    for k in range(DE // P):
                        if k % 2 == 0:
                            pe.wait_ge(wd_in[k // 2], (i + 1) * 16)
                        for h in range(2):
                            mm = pe.matmul(ps_y[h][:], hidT[:, k, :], wd[:, k, h * 512:(h + 1) * 512], start=(k == 0),
                                           stop=(k == DE // P - 1))
                        if k % 2:
                            mm.then_inc(y_ps, 1)

                def turn_hidden(i):
                    pe.wait_ge(hid_done, i + 1)
                    for k in range(DE // P):
                        mm = pe.transpose(ps_h[:, k * P:(k + 1) * P], hid[:, k * P:(k + 1) * P], ident)
                    mm.then_inc(h_ps, 1)

                pe.sem_inc(y_ps, 4)
                turn_x(0)
                gate_up(0)
                turn_x(1)
                turn_hidden(0)
                with pe.Fori(1, n) as i:
                    gate_up(i)
                    turn_x(i + 1)
                    pe.wait_ge(yo_done, i * 2)
                    down(i - 1)
                    turn_hidden(i)
                pe.wait_ge(yo_done, n * 2)
                down(n - 1)

            @block.scalar
            def _(act):
                n = blocks(act)

                def squares(i):
                    act.wait_ge(x_in, (i + 1) * 16)
                    act.activation(junk, xg, ACT.Square, accum_out=ss).then_inc(ss_done, 1)

                def tanh(i):
                    act.wait_ge(g_ps, i * 2 + 2)
                    act.wait_ge(rs_done, i + 1)
                    act.activation(th, ps_g[:], ACT.Tanh, scale=hrs).then_inc(tanh_done, 1)

                def hidden(i):
                    act.wait_ge(h_ps, i + 1)
                    act.activation(hidT, ps_h[:].rearrange("p (k q) -> p k q", k=DE // P), ACT.Copy).then_inc(hidT_done, 1)

                def split_hi(i, w, h):
                    act.wait_ge(w_in[w][h], (i + 1) * 16)
                    if not isinstance(i, int) or i:
                        act.wait_ge({"g": g_ps, "u": u_ps}[w], i * 2 + (h - 1))
                    act.activation(hi[w][:, 4 * h:4 * h + 4, :], raw[w][:, 4 * h:4 * h + 4, :], ACT.Copy).then_inc(hi_done[w], 1)

                def x_hi(i):
                    act.wait_ge(xT_done, i * 2 + 2)
                    act.activation(xT_hi, xT, ACT.Copy).then_inc(x_hi_done, 1)

                split_hi(0, "g", 0)
                split_hi(0, "g", 1)
                squares(0)
                x_hi(0)
                split_hi(0, "u", 0)
                split_hi(0, "u", 1)
                split_hi(1, "g", 0)
                tanh(0)
                split_hi(1, "g", 1)
                act.wait_ge(ss_done, 1)
                squares(1)
                x_hi(1)
                split_hi(1, "u", 0)
                split_hi(1, "u", 1)
                hidden(0)
                with act.Fori(1, n) as i:
                    split_hi(i + 1, "g", 0)
                    tanh(i)
                    split_hi(i + 1, "g", 1)
                    act.wait_ge(ss_done, i + 1)
                    squares(i + 1)
                    split_hi(i + 1, "u", 0)
                    x_hi(i + 1)
                    split_hi(i + 1, "u", 1)
                    act.wait_ge(y_ps, i * 2 + 4)
                    hidden(i)

            @block.vector
            def _(dve):
                n = blocks(dve)
                dve.sem_inc(yo_done, 2)

                def copy_x(i):
                    for b in range(2):
                        dve.wait_ge(x_ps, i * 2 + (b + 1))
                        dve.tensor_tensor(xT[:, 4 * b:4 * b + 4, :], ps_x[b][:].rearrange("p (k q) -> p k q", k=4),
                                          g_ffn[:, 4 * b:4 * b + 4].unsqueeze(2).to_broadcast([P, 4, P]),
                                          ALU.mult).then_inc(xT_done, 1)

                def glu(i):
                    dve.wait_ge(tanh_done, i + 1)
                    dve.scalar_tensor_tensor(out=th, in0=th, scalar=1.0, in1=ps_g[:], op0=ALU.add, op1=ALU.mult).then_inc(glu_done, 1)
                    dve.wait_ge(glu_done, i + 1)
                    dve.wait_ge(u_ps, i * 2 + 2)
                    dve.scalar_tensor_tensor(out=hid, in0=th, scalar=hrs2, in1=ps_u[:], op0=ALU.mult, op1=ALU.mult).then_inc(hid_done, 1)

                def weigh(i):
                    dve.wait_ge(y_ps, i * 2 + 6)
                    dve.wait_ge(shifted, i + 1)
                    for h in range(2):
                        dve.tensor_scalar(yo[:, h * 512:(h + 1) * 512], ps_y[h][:], prv[:, 1:2], None, ALU.mult).then_inc(yo_done, 1)

                def x_lo(i):
                    dve.wait_ge(x_hi_done, i + 1)
                    dve.tensor_tensor(xT_lo, xT, xT_hi.bitcast(F32), ALU.subtract).then_inc(x_lo_done, 1)

                split_lo = lo_splitter(dve, raw, hi, lo, hi_done, lo_done)
                split_lo(0, "g", 0)
                split_lo(0, "g", 1)
                copy_x(0)
                x_lo(0)
                split_lo(1, "g", 0)
                glu(0)
                copy_x(1)
                x_lo(1)
                split_lo(1, "g", 1)
                with dve.Fori(1, n) as i:
                    split_lo(i + 1, "g", 0)
                    glu(i)
                    copy_x(i + 1)
                    x_lo(i + 1)
                    split_lo(i + 1, "g", 1)
                    weigh(i - 1)
                weigh(n - 1)

            @block.gpsimd
            def _(pool):
                pool.memset(half, -0.5).then_inc(set_done, 1)
                n = blocks(pool)
                pool.wait_ge(set_done, 1)

                def entry(i):
                    return slots[:, i, :] if isinstance(i, int) else slots[:, bass.ds(i, 1), :].rearrange("p o c -> p (o c)")

                def gather(i, copied):
                    pool.tensor_copy(nxt, entry(i)).then_inc(pstep, 1)
                    pool.wait_ge(pstep, copied)
                    pool.sem_inc(settled, 1)
                    pool.indirect_dma_start(xg, None, a["x2s"], bass.IndirectOffsetOnAxis(ap=nxt[:, 0:1].bitcast(I32), axis=0)).then_inc(x_in, 16)

                def root(i, link):
                    pool.wait_ge(ss_done, i + 1)
                    pool.sem_inc(settled, 1)
                    pool.tensor_scalar(ms, ss, 1.0 / D, EPS, ALU.mult, ALU.add).then_inc(pstep, 1)
                    pool.wait_ge(pstep, link(1))
                    pool.tensor_tensor(rs, ms, half, ALU.pow).then_inc(pstep, 1)
                    pool.wait_ge(pstep, link(2))
                    pool.sem_inc(settled, 1)
                    pool.tensor_scalar(hrs, rs, 0.5, 1.0, ALU.mult, ALU.mult).then_inc(pstep, 1)
                    pool.wait_ge(pstep, link(3))
                    pool.tensor_tensor(hrs2, hrs, rs, ALU.mult).then_inc(rs_done, 1)

                def scatter():
                    pool.indirect_dma_start(a["y"], bass.IndirectOffsetOnAxis(ap=prv[:, 0:1].bitcast(I32), axis=0), yo, None,
                                            compute_op=ALU.add).then_inc(y_out, 16)

                split_lo = lo_splitter(pool, raw, hi, lo, hi_done, lo_done)
                gather(0, 1)
                pool.tensor_copy(prv, entry(NTAB - 1))
                pool.memset(yo, 0.0).then_inc(pstep, 1)
                pool.wait_ge(pstep, 2)
                scatter()
                root(0, lambda k: 2 + k)
                pool.wait_ge(x_ps, 2)
                pool.wait_ge(x_in, 16)
                gather(1, 6)
                split_lo(0, "u", 0)
                split_lo(0, "u", 1)
                pool.wait_ge(hid_done, 1)
                root(1, lambda k: 6 + k)
                pool.wait_ge(x_ps, 4)
                gather(2, 10)
                split_lo(1, "u", 0)
                split_lo(1, "u", 1)
                with pool.Fori(1, n) as i:
                    split_lo(i + 1, "u", 0)
                    pool.wait_ge(y_out, i * 16)
                    pool.sem_inc(settled, 1)
                    pool.tensor_copy(prv, entry(i - 1)).then_inc(shifted, 1)
                    pool.wait_ge(hid_done, i + 1)
                    root(i + 1, lambda k: i * 4 + (6 + k))
                    pool.wait_ge(x_ps, i * 2 + 4)
                    pool.wait_ge(x_in, i * 16 + 32)
                    pool.sem_inc(settled, 1)
                    gather(i + 2, i * 4 + 10)
                    split_lo(i + 1, "u", 1)
                    pool.wait_ge(shifted, i)
                    pool.wait_ge(yo_done, i * 2 + 2)
                    pool.sem_inc(settled, 1)
                    scatter()
                pool.wait_ge(x_in, n * 16 + 32)
                pool.wait_ge(y_out, n * 16)
                pool.sem_inc(settled, 1)
                pool.tensor_copy(prv, entry(n - 1)).then_inc(shifted, 1)
                pool.wait_ge(shifted, n)
                pool.wait_ge(yo_done, n * 2 + 2)
                pool.sem_inc(settled, 1)
                scatter()
                pool.wait_ge(y_out, n * 16 + 16)


_WEIGHTS = ["norm_mix_g", "w_in", "norm_v_g", "w_spatial", "b_spatial", "q_norm_g", "k_norm_g", "sink", "w_proj_a",
            "w_proj_b", "w_out", "norm_ffn_g", "w_router_group", "b_router_group", "w_router_expert",
            "b_router_expert", "w_gate_e", "w_up_e", "w_down_e"]


def tables():
    half = HD // 2
    inv = (np.float32(10000.0) ** (-np.arange(half, dtype=np.float32) / np.float32(half))).astype(np.float32)
    rope = np.zeros((NG + 1, P, 5, 2, half), np.float32)
    mask = np.zeros((NG + 1, P, 3, 3 * P), np.float32)
    q, k = np.arange(P)[:, None], np.arange(3 * P)[None, :] - P
    band = np.abs(k - q) <= P
    for g in range(NG + 1):
        start = max(g - 1, 0) * G
        length = S_PROMPT if g == 0 else S_SAMPLE
        for t in range(5):
            ang = (start + t * P + np.arange(P)).astype(np.float32)[:, None] * inv[None, :]
            rope[g, :, t, 0], rope[g, :, t, 1] = np.cos(ang), np.sin(ang)
        for m, block in enumerate((0, 1, GT - 1)):
            pos = start + block * P + k
            mask[g, :, m] = np.where(band & (pos >= 0) & (pos < length), 0.0, NEG)
    counts = np.stack([np.arange(EPG), np.arange(EPG) - 100]).astype(np.float32)
    return {"counts": counts.reshape(1, -1), "row": np.arange(P, dtype=np.float32)[None, :],
            "ids": np.ascontiguousarray(np.arange(T, dtype=np.float32).reshape(NT, P).T),
            "upper": np.triu(np.ones((P, P), np.float32), 1), "ident": np.eye(P, dtype=np.float32), "rope": rope.reshape((NG + 1) * P, -1),
            "mask": mask.reshape((NG + 1) * P, -1)}


def kernel(x_prompt, x_sample, **weights):
    import concourse.bacc as bacc
    from concourse.bass_utils import run_bass_kernel_spmd

    xp, xs = np.asarray(x_prompt)[0], np.asarray(x_sample)[0]
    w = {name: np.asarray(weights[name])[0] for name in _WEIGHTS}
    arrays = {"x_all": np.concatenate([xp, xs, xp, xs[:P]])}
    arrays.update(tables())
    for name in ("norm_mix_g", "norm_v_g", "norm_ffn_g"):
        w[name] = np.ascontiguousarray(w[name].reshape(KT, P).T)
    for name in ("q_norm_g", "k_norm_g", "sink", "b_router_group", "b_router_expert"):
        w[name] = w[name][None, :]
    w["b_spatial"] = w["b_spatial"].reshape(1, -1)
    arrays.update(w)
    nc = bacc.Bacc("TRN2", target_bir_lowering=False, num_devices=1, dynamic_dma_scratch_size=4096)
    a = {}
    for name in arrays:
        arrays[name] = np.ascontiguousarray(arrays[name])
        a[name] = nc.dram_tensor(name, arrays[name].shape, mybir.dt.from_np(arrays[name].dtype), kind="ExternalInput").ap()
    a["y"] = nc.dram_tensor("y", (T + P, D), F32, kind="ExternalOutput").ap()
    a["x2s"] = nc.dram_tensor("x2s", (T + P, D), F32, kind="Internal").ap()
    a["table"] = nc.dram_tensor("table", (1, NTAB * TW), I32, kind="Internal").ap()
    build(nc, a)
    y = run_bass_kernel_spmd(nc, [arrays], core_ids=[0]).results[0]["y"]
    return y[None, :S_PROMPT], y[None, S_PROMPT:T]


def build(nc, a):
    mixers(nc, a)
    with ExitStack() as ctx:
        held = {}
        for name, shape, dt in (("wg", [P, KT, DE], F32), ("wu", [P, KT, DE], F32), ("wd", [P, DE // P, D], F32),
                                ("slots", [P, NTAB, 2], F32), ("ident", [P, P], F32), ("g_ffn", [P, KT], F32), ("tab", [1, NTAB * TW], I32)):
            held[name] = ctx.enter_context(nc.sbuf_tensor("held_" + name, shape, dt))[...]
        held["tab_in"] = ctx.enter_context(nc.semaphore("tab_in"))
        for w in ("wg", "wu", "wd"):
            held[w + "_in"] = [ctx.enter_context(nc.semaphore(f"{w}_in{h}")) for h in range(2)]
        route(nc, a, held)
        experts(nc, a, held)
```
